# Optimizing a Trainium2 kernel written in Bass

```python
import jax, jax.numpy as jnp
from jax import lax
import numpy as np

D_MODEL = 1024
BATCH = 1
SEQ = 1024
DEPTH = 1

GLA_HEADS = 4
GLA_DK = 128
GLA_DV = 256
GLA_KEY = GLA_HEADS * GLA_DK
GLA_VAL = GLA_HEADS * GLA_DV
GLA_GATE_RANK = 16
GLA_GATE_NORM = 16.0
GLA_CHUNK = 64
LRU_WIDTH = 1344
LRU_BLOCKS = 8
LRU_BW = LRU_WIDTH // LRU_BLOCKS
LRU_CONV = 4
LRU_C = 8.0
LRU_MIN_RAD = 0.9
LRU_MAX_RAD = 0.999
D_FF = 3 * D_MODEL
FFN_CONV = 3
EPS = 1e-6

D_PROJ = 2 * GLA_KEY + 2 * GLA_VAL + GLA_GATE_RANK + 2 * LRU_WIDTH + 2 * D_MODEL

kernel_name = "hybrid_gla_rglru_convffn"

def rms_norm(x, g):
    xf = x.astype(jnp.float32)
    y = xf * lax.rsqrt(jnp.mean(xf * xf, axis=-1, keepdims=True) + EPS)
    return (y * g.astype(jnp.float32)).astype(x.dtype)

def causal_dwconv(x, w, b):
    K = w.shape[0]
    S = x.shape[1]
    xp = jnp.pad(x, ((0, 0), (K - 1, 0), (0, 0)))
    y = b
    for j in range(K):
        y = y + xp[:, j:j + S] * w[j]
    return y

def gla_chunked(q, k, v, gk):
    B, S, H, dk = q.shape
    dv = v.shape[-1]
    C = GLA_CHUNK
    N = S // C
    out_dtype = v.dtype

    def to_chunks(t):
        return t.astype(jnp.float32).reshape(B, N, C, H, -1).transpose(0, 3, 1, 2, 4)

    qc = to_chunks(q) * (dk ** -0.5)
    kc = to_chunks(k)
    vc = to_chunks(v)
    b = jnp.cumsum(to_chunks(gk), axis=3)
    b_last = b[:, :, :, -1:]
    q_t = qc * jnp.exp(b)
    k_t = kc * jnp.exp(-b)
    k_s = kc * jnp.exp(b_last - b)

    mask = jnp.tril(jnp.ones((C, C), dtype=bool))
    A = jnp.einsum('bhnik,bhnjk->bhnij', q_t, k_t)
    A = jnp.where(mask, A, 0.0)
    o_intra = jnp.einsum('bhnij,bhnjv->bhniv', A, vc)

    dS = jnp.einsum('bhnck,bhncv->bhnkv', k_s, vc)
    decay = jnp.exp(b_last[:, :, :, 0])

    def step(s_prev, inp):
        d, ds = inp
        return d[..., None] * s_prev + ds, s_prev

    s0 = jnp.zeros((B, H, dk, dv), jnp.float32)
    _, s_start = lax.scan(step, s0, (jnp.moveaxis(decay, 2, 0), jnp.moveaxis(dS, 2, 0)))
    s_start = jnp.moveaxis(s_start, 0, 2)
    o_inter = jnp.einsum('bhnck,bhnkv->bhncv', q_t, s_start)

    o = o_intra + o_inter
    return o.transpose(0, 2, 3, 1, 4).reshape(B, S, H, dv).astype(out_dtype)

def rg_lru(x, w_a, b_a, w_x, b_x, a_param):
    B, S, W = x.shape
    xf = x.astype(jnp.float32)
    xb = xf.reshape(B, S, LRU_BLOCKS, LRU_BW)
    r = jax.nn.sigmoid(jnp.einsum('bsnc,ncd->bsnd', xb, w_a.astype(jnp.float32)).reshape(B, S, W) + b_a)
    i = jax.nn.sigmoid(jnp.einsum('bsnc,ncd->bsnd', xb, w_x.astype(jnp.float32)).reshape(B, S, W) + b_x)
    log_a = -LRU_C * r * jax.nn.softplus(a_param.astype(jnp.float32))
    a = jnp.exp(log_a)
    u = jnp.sqrt(-jnp.expm1(2.0 * log_a)) * (i * xf)

    def combine(c1, c2):
        a1, b1 = c1
        a2, b2 = c2
        return a1 * a2, a2 * b1 + b2

    _, h = lax.associative_scan(combine, (a, u), axis=1)
    return h.astype(x.dtype)

def setup_inputs(seed: int = 0) -> dict:
    key = jax.random.key(seed)
    ks = jax.random.split(key, 24)
    L = DEPTH

    def nrm(k, shape, fan_in):
        return jax.random.normal(k, shape, jnp.float32) * (fan_in ** -0.5)

    def gain(k, shape):
        return 1.0 + 0.02 * jax.random.normal(k, shape, jnp.float32)

    def small(k, shape):
        return 0.01 * jax.random.normal(k, shape, jnp.float32)

    x = jax.random.normal(ks[0], (BATCH, SEQ, D_MODEL), jnp.float32)
    rad = jax.random.uniform(ks[13], (L, LRU_WIDTH), jnp.float32, LRU_MIN_RAD, LRU_MAX_RAD)
    lru_a_param = jnp.log(jnp.expm1(-jnp.log(rad)))
    return {
        "x": x,
        "attn_norm": gain(ks[1], (L, D_MODEL)),
        "w_in": nrm(ks[2], (L, D_MODEL, D_PROJ), D_MODEL),
        "gla_wf2": nrm(ks[3], (L, GLA_GATE_RANK, GLA_KEY), GLA_GATE_RANK),
        "gla_bf2": small(ks[4], (L, GLA_KEY)),
        "gla_onorm": gain(ks[5], (L, GLA_DV)),
        "gla_wo": nrm(ks[6], (L, GLA_VAL, D_MODEL), GLA_VAL),
        "lru_conv_w": nrm(ks[7], (L, LRU_CONV, LRU_WIDTH), LRU_CONV),
        "lru_conv_b": small(ks[8], (L, LRU_WIDTH)),
        "lru_wa": nrm(ks[9], (L, LRU_BLOCKS, LRU_BW, LRU_BW), LRU_BW),
        "lru_ba": small(ks[10], (L, LRU_WIDTH)),
        "lru_wx": nrm(ks[11], (L, LRU_BLOCKS, LRU_BW, LRU_BW), LRU_BW),
        "lru_bx": small(ks[12], (L, LRU_WIDTH)),
        "lru_a_param": lru_a_param,
        "lru_wo": nrm(ks[14], (L, LRU_WIDTH, D_MODEL), LRU_WIDTH),
        "w_out": nrm(ks[15], (L, D_MODEL, D_MODEL), D_MODEL),
        "ffn_norm": gain(ks[16], (L, D_MODEL)),
        "ffn_wup": nrm(ks[17], (L, D_MODEL, 2 * D_FF), D_MODEL),
        "ffn_conv_w": nrm(ks[18], (L, FFN_CONV, 2 * D_FF), FFN_CONV),
        "ffn_conv_b": small(ks[19], (L, 2 * D_FF)),
        "ffn_wdown": nrm(ks[20], (L, D_FF, D_MODEL), D_FF),
        "final_norm": gain(ks[21], (D_MODEL,)),
    }

def reference(x, attn_norm, w_in, gla_wf2, gla_bf2, gla_onorm, gla_wo,
              lru_conv_w, lru_conv_b, lru_wa, lru_ba, lru_wx, lru_bx, lru_a_param, lru_wo,
              w_out, ffn_norm, ffn_wup, ffn_conv_w, ffn_conv_b, ffn_wdown, final_norm):
    B, S, _ = x.shape
    splits = np.cumsum([GLA_KEY, GLA_KEY, GLA_VAL, GLA_VAL, GLA_GATE_RANK,
                        LRU_WIDTH, LRU_WIDTH, D_MODEL])
    for l in range(DEPTH):
        h = rms_norm(x, attn_norm[l])
        p = jnp.einsum('bsd,de->bse', h, w_in[l])
        q, k, v, g, f_low, x_lru, lru_gate, gate_a, gate_b = jnp.split(p, splits, axis=-1)

        gk = jax.nn.log_sigmoid(
            (jnp.einsum('bsr,rk->bsk', f_low, gla_wf2[l]) + gla_bf2[l]).astype(jnp.float32)) / GLA_GATE_NORM
        o = gla_chunked(q.reshape(B, S, GLA_HEADS, GLA_DK),
                        k.reshape(B, S, GLA_HEADS, GLA_DK),
                        v.reshape(B, S, GLA_HEADS, GLA_DV),
                        gk.reshape(B, S, GLA_HEADS, GLA_DK))
        o = rms_norm(o, gla_onorm[l]) * jax.nn.silu(g.reshape(B, S, GLA_HEADS, GLA_DV))
        y_a = jnp.einsum('bse,ed->bsd', o.reshape(B, S, GLA_VAL), gla_wo[l])

        xc = causal_dwconv(x_lru, lru_conv_w[l], lru_conv_b[l])
        hl = rg_lru(xc, lru_wa[l], lru_ba[l], lru_wx[l], lru_bx[l], lru_a_param[l])
        y_b = jnp.einsum('bse,ed->bsd', hl * jax.nn.gelu(lru_gate, approximate=True), lru_wo[l])

        merged = jax.nn.sigmoid(gate_a) * y_a + jax.nn.sigmoid(gate_b) * y_b
        x = x + jnp.einsum('bsd,de->bse', merged, w_out[l])

        h = rms_norm(x, ffn_norm[l])
        u = jnp.einsum('bsd,df->bsf', h, ffn_wup[l])
        u = causal_dwconv(u, ffn_conv_w[l], ffn_conv_b[l])
        u_gate, u_val = jnp.split(u, 2, axis=-1)
        x = x + jnp.einsum('bsf,fd->bsd', jax.nn.gelu(u_gate, approximate=True) * u_val, ffn_wdown[l])

    return rms_norm(x, final_norm)


_drawn_inputs = setup_inputs


def setup_inputs(seed=0):
    import zlib

    import numpy as np

    out = dict(_drawn_inputs(seed))
    spreads = {}
    factors = {'attn_norm': 3.349,
     'gla_bf2': 8.0,
     'gla_onorm': 7.852,
     'lru_conv_b': 6.166,
     'lru_ba': 64.0,
     'lru_bx': 64.0,
     'ffn_norm': 11.865,
     'ffn_conv_b': 23.237,
     'final_norm': 7.532}
    for name, (base, spread) in spreads.items():
        noise = np.random.default_rng([zlib.crc32(name.encode()), seed]).standard_normal(out[name].shape)
        drawn = base * np.exp(spread * noise) if base else spread * noise
        out[name] = __import__('jax').numpy.asarray(drawn.astype(out[name].dtype))
    for name, factor in factors.items():
        out[name] = (out[name] * factor).astype(out[name].dtype)
    return out
```

```python
from contextlib import ExitStack

import concourse.bass as bass
from concourse import mybir

F32 = mybir.dt.float32
F32R = mybir.dt.float32r
ALU = mybir.AluOpType
ACT = mybir.ActivationFunctionType

P = 128
D = 1024
S = 1024
KD = D // P
HALF = 512
EPS = 1e-6

HEADS, DK, DV, CHUNK = 4, 128, 256, 64
RANK = 16
PAIRS = S // P
GATE_NORM = 16.0
LW = 1344
BW = LW // 8
LT = 112
LTILES = LW // LT
LGROUPS = LTILES // 3
FF = 3 * D
FT = FF // P

C_Q = 0
C_K = C_Q + HEADS * DK
C_V = C_K + HEADS * DK
C_G = C_V + HEADS * DV
C_F = C_G + HEADS * DV
C_LX = C_F + RANK
C_LG = C_LX + LW
C_GA = C_LG + LW
C_GB = C_GA + D

U_F = 0
U_QKV0 = 1
U_HEAD = U_QKV0 + 4
U_G3 = U_HEAD + 6 * (HEADS - 1)
U_YA = U_G3 + 2
U_LRU = U_YA + 2 * KD
U_GB = U_LRU + 8 * LGROUPS
U_YB = U_GB + KD
U_OUT = U_YB + 2 * KD
U_UP = U_OUT + 2 * KD
U_DN = U_UP + 2 * FT
U_END = U_DN + 2 * FT

A_NORM, A_BF2, A_ONORM, A_FNORM, A_FB, A_W2 = 0, 8, 12, 14, 22, 70
N_A = A_W2 + 2 * FT
N_B = 4 * FT
L_W, L_B, L_BA, L_BX, L_AP = 0, 4 * LTILES, 5 * LTILES, 6 * LTILES, 7 * LTILES
N_L = 8 * LTILES


class Unit:

    def __init__(self, const, per=0, i=None, extra=(0, 0), apart=(0, 0)):
        self.const, self.per, self.i, self.extra, self.apart = const, per, i, extra, apart

    def __add__(self, n):
        return Unit(self.const + n, self.per, self.i, self.extra, self.apart)

    def value(self, const, per):
        return const if self.i is None else self.i * per + const

    def slot(self):
        return self.const % 2

    def done(self, n=1):
        return self.value(self.const + n, self.per)

    def loaded(self):
        return self.value(16 * (self.const // 2 + 1 + 3 * self.extra[0]), 8 * self.per + 48 * self.extra[1])

    def ps(self, n=0):
        return self.value(self.const // 2 + n - self.apart[0], self.per // 2 - self.apart[1])


def lru_unit(g, r):
    return Unit(U_LRU + r, 8, g, extra=(int(r >= 6), 1), apart=(int(r >= 8), 1))


def ffn_unit(j):
    apart = LGROUPS + 2 * KD
    return late_unit(U_UP + 2 * j, apart=apart) if isinstance(j, int) else late_unit(U_UP, 2, j, apart=apart)


def gb_uses(slot):
    return sum(1 for u in range(U_YB) if u % 2 == slot) - LGROUPS


def late_unit(const, per=0, i=None, apart=LGROUPS):
    return Unit(const, per, i, extra=(LGROUPS, 0), apart=(apart, 0))


class Order:

    def __init__(self, eng, sem):
        self.eng, self.sem, self.base, self.n = eng, sem, 0, 0

    def after(self, ins):
        ins.then_inc(self.sem, 1)
        self.n += 1
        self.eng.wait_ge(self.sem, self.base + self.n)

    def enter(self, i, per):
        self.saved = (self.base, self.n, per)
        self.base, self.n = i * per + (self.base + self.n), 0

    def leave(self, times):
        base, n, per = self.saved
        assert self.n == per, (self.n, per)
        self.base, self.n = base + n + per * times, 0


def build(nc, x, attn_norm, w_in, gla_wf2, gla_bf2, gla_onorm, gla_wo, lru_conv_w, lru_conv_b,
          lru_wa, lru_ba, lru_wx, lru_bx, lru_a_param, lru_wo, w_out, ffn_norm, ffn_wup,
          ffn_conv_w, ffn_conv_b, ffn_wdown, final_norm, out):
    ds = bass.ds
    ctx = ExitStack()
    with ctx:
        def sb(name, shape, dt=F32, scope=ctx):
            return scope.enter_context(nc.sbuf_tensor(name, shape, dt))

        def sem(name):
            return ctx.enter_context(nc.semaphore(name))

        vec_a = sb("vec_a", [P, N_A])
        vec_b = sb("vec_b", [P, N_B])
        vec_l = sb("vec_l", [LT, N_L])
        ident = sb("ident", [P, P])
        causal = sb("causal", [P, P])
        ones = sb("ones", [P, CHUNK])
        onorm_half = sb("onorm_half", [P, 2])
        sp2 = sb("sp2", [LT, LTILES])
        minus_sp4 = sb("minus_sp4", [LT, LTILES])
        half_b = sb("half_b", [LT, 2 * LTILES])
        soft = sb("soft", [LT, 4, LTILES])
        sumsq = sb("sumsq", [P, 8])
        ms = sb("ms", [P, 8])
        rs = sb("rs", [P, 8])
        newton = sb("newton", [P, 8])
        wf_raw = sb("wf_raw", [RANK, HEADS * DK])
        w_raw = sb("w_raw", [P, 2, 1024])
        w_hi = sb("w_hi", [P, 2, 1024], F32R)
        w_lo = sb("w_lo", [P, 2, 1024], F32R)

        h_scope = ExitStack()
        h_hi = sb("h_hi", [P, KD, S], F32R, h_scope)
        h_lo = sb("h_lo", [P, KD, S], F32R, h_scope)

        xs = ExitStack()
        x_in = sb("x_in", [P, KD, S], scope=xs)
        xn1 = sb("xn1", [P, 2, S], scope=xs)
        xr1 = sb("xr1", [P, 2, S], scope=xs)
        rows_a = sb("rows_a", [N_A, P], scope=xs)
        rows_b = sb("rows_b", [N_B, P], scope=xs)
        rows_l = sb("rows_l", [N_L, LT], scope=xs)
        xs.close()

        og_scope = ExitStack()
        og_raw = sb("og_raw", [P, KD, S], scope=og_scope)
        gla = ExitStack()
        f_hi = sb("f_hi", [RANK, S], F32R, gla)
        f_lo = sb("f_lo", [RANK, S], F32R, gla)
        wf_hi = sb("wf_hi", [RANK, DK], F32R, gla)
        wf_lo = sb("wf_lo", [RANK, DK], F32R, gla)
        q_hi = sb("q_hi", [P, PAIRS * 256 + P], F32R, gla)
        q_lo = sb("q_lo", [P, PAIRS * 256 + P], F32R, gla)
        k_hi = sb("k_hi", [P, S], F32R, gla)
        k_lo = sb("k_lo", [P, S], F32R, gla)
        cum = sb("cum", [P, S], scope=gla)
        g1 = sb("g1", [P, S], scope=gla)
        g2 = sb("g2", [P, S], scope=gla)
        ks = sb("ks", [P, S], scope=gla)
        vo = sb("vo", [P, PAIRS, DV], scope=gla)
        sg = sb("sg", [P, 2, S], scope=gla)
        decay = sb("decay", [P, S // CHUNK], scope=gla)
        kt_hi = sb("kt_hi", [P, 2, P], F32R, gla)
        kt_lo = sb("kt_lo", [P, 2, P], F32R, gla)
        v_hi = sb("v_hi", [P, 2, DV], F32R, gla)
        v_lo = sb("v_lo", [P, 2, DV], F32R, gla)
        at_raw = sb("at_raw", [P, P], scope=gla)
        at_hi = sb("at_hi", [P, P], F32R, gla)
        at_lo = sb("at_lo", [P, P], F32R, gla)
        s_raw = sb("s_raw", [P, DV], scope=gla)
        s_hi = sb("s_hi", [P, 2, DV], F32R, gla)
        s_lo = sb("s_lo", [P, 2, DV], F32R, gla)
        squares = sb("squares", [P, DV], scope=gla)
        gla.close()
        og_scope.close()
        ya = ExitStack()
        og_lo = sb("og_lo", [P, KD, S], F32R, ya)
        og_hi = sb("og_hi", [P, KD, S], F32R, ya)
        m_a = sb("m_a", [P, KD, S], scope=ya)
        t_a = sb("t_a", [P, S], scope=ya)
        ya.close()
        lru = ExitStack()
        hl = sb("hl", [LT, LTILES, S], scope=lru)
        xc_hi = sb("xc_hi", [LT, 3, S], F32R, lru)
        xc_lo = sb("xc_lo", [LT, 3, S], F32R, lru)
        conv = sb("conv", [LT, S], scope=lru)
        lw = sb("lw", [LT, 3, S], scope=lru)
        la = sb("la", [LT, 3, S], scope=lru)
        lc = sb("lc", [LT, 3, S], scope=lru)
        lru.close()
        mg = ExitStack()
        hl_lo = sb("hl_lo", [LT, LTILES, S], F32R, mg)
        t_b = sb("t_b", [P, KD, S], scope=mg)
        m = sb("m", [P, KD, S], scope=mg)
        mg.close()
        oscope = ExitStack()
        x2 = sb("x2", [P, KD, S], scope=oscope)
        xn2 = sb("xn2", [P, 2, S], scope=oscope)
        xr2 = sb("xr2", [P, 2, S], scope=oscope)
        oscope.close()
        fscope = ExitStack()
        hid = sb("hid", [P, FT, S], scope=fscope)
        ug = sb("ug", [P, S], scope=fscope)
        uv = sb("uv", [P, S], scope=fscope)
        ad_hi = sb("ad_hi", [P, 2, HALF], F32R, fscope)
        ad_lo = sb("ad_lo", [P, 2, HALF], F32R, fscope)
        fscope.close()

        h_scope.close()
        h2 = ExitStack()
        hl_hi = sb("hl_hi", [LT, LTILES, S], F32R, h2)
        yb = sb("yb", [P, S], scope=h2)
        ao_hi = sb("ao_hi", [P, 2, HALF], F32R, h2)
        ao_lo = sb("ao_lo", [P, 2, HALF], F32R, h2)
        h2.close()
        h3 = ExitStack()
        g_hi = sb("g_hi", [P, KD, S], F32R, h3)
        g_lo = sb("g_lo", [P, KD, S], F32R, h3)
        h3.close()
        h4 = ExitStack()
        y = sb("y", [P, KD, S], scope=h4)
        final_gain = sb("final_gain", [P, D], scope=h4)
        junk = sb("junk", [P, S], scope=h4)
        h4.close()

        pp = [ctx.enter_context(nc.psum_tensor(f"pp{i}", [P, 1024], F32)) for i in range(4)]
        at_ps, o_ps = pp[2][:, 0:P], pp[2][:, HALF:HALF + DV]
        tr_ps, ds_ps = pp[3][:, 0:P + DV], pp[3][:, HALF:2 * HALF]

        m_dram = nc.dram_tensor("m_scratch", [P, KD, S], F32, kind="Internal").ap()
        x2_dram = nc.dram_tensor("x2_scratch", [P, KD, S], F32, kind="Internal").ap()

        w_rounded = sem("w_rounded")
        w_split = sem("w_split")
        unit_done = sem("unit_done")
        zeroed = sem("zeroed")
        act_order = sem("act_order")
        dve_order = sem("dve_order")
        setup = sem("setup")
        rows_loaded = sem("rows_loaded")
        vecs_T = sem("vecs_T")
        vecs = sem("vecs")
        soft_abs = sem("soft_abs")
        soft_e = sem("soft_e")
        squared = sem("squared")
        ms_ready = sem("ms_ready")
        rs0_ready = sem("rs0_ready")
        xn_ready = sem("xn_ready")
        xT_ready = sem("xT_ready")
        xr_ready = sem("xr_ready")
        xr_rounded = sem("xr_rounded")
        xT_split = sem("xT_split")
        wf_ready = sem("wf_ready")
        z_ready = sem("z_ready")
        z_abs = sem("z_abs")
        z_free = sem("z_free")
        sp_ready = sem("sp_ready")
        cum_ready = sem("cum_ready")
        bdiff_ready = sem("bdiff_ready")
        gates_ready = sem("gates_ready")
        qk_rounded = sem("qk_rounded")
        qk_split = sem("qk_split")
        v_stored = sem("v_stored")
        tr_ready = sem("tr_ready")
        kv_rounded = sem("kv_rounded")
        kv_split = sem("kv_split")
        at_ready = sem("at_ready")
        at_masked = sem("at_masked")
        at_rounded = sem("at_rounded")
        at_split = sem("at_split")
        ds_ready = sem("ds_ready")
        s_cleared = sem("s_cleared")
        s_updated = sem("s_updated")
        s_rounded = sem("s_rounded")
        s_split = sem("s_split")
        o_ready = sem("o_ready")
        o_stored = sem("o_stored")
        g_tanh = sem("g_tanh")
        on_ready = sem("on_ready")
        oT_ready = sem("oT_ready")
        og_ready = sem("og_ready")
        og_rounded = sem("og_rounded")
        og_split = sem("og_split")
        m_stored = sem("m_stored")
        m_loaded = sem("m_loaded")
        m_ready = sem("m_ready")
        xc_split = sem("xc_split")
        ra_ready = sem("ra_ready")
        rx_ready = sem("rx_ready")
        ra_free = sem("ra_free")
        rx_free = sem("rx_free")
        gated = sem("gated")
        lru_act = sem("lru_act")
        lru_out = sem("lru_out")
        hl_rounded = sem("hl_rounded")
        hl_split = sem("hl_split")
        a_rounded = sem("a_rounded")
        a_split = sem("a_split")
        acc_ready = sem("acc_ready")
        acc_stored = sem("acc_stored")
        xres_loaded = sem("xres_loaded")
        x2_saved = sem("x2_saved")
        x2_loaded = sem("x2_loaded")
        u_first = sem("u_first")
        u_gelu = sem("u_gelu")
        hid_ready = sem("hid_ready")
        y_ready = sem("y_ready")
        out_saved = sem("out_saved")
        slots_freed, gate_slots_freed = sem("slots_freed"), sem("gate_slots_freed")
        w_loaded = [sem("w_loaded0"), sem("w_loaded1")]
        ps_free = [sem("ps_free0"), sem("ps_free1")]
        yb_free = [sem("yb_free0"), sem("yb_free1")]
        x_loaded = [sem(f"x_loaded{i}") for i in range(KD)]

        block = ctx.enter_context(nc.Block())

        def gla_q(t, p, c):
            return t[:, p * 256 + c * P:p * 256 + (c + 1) * P]

        def gla_q_tokens(t, p):
            return t[:, p * 256:p * 256 + 384].rearrange("a (c x) -> a c x", x=192)[:, :, 0:CHUNK]

        def q_chunks(t, c):
            return t[:, 0:PAIRS * 256].rearrange("a (p x) -> a p x", x=256)[
                :, :, c * 192:c * 192 + CHUNK]

        def chunks(t, c):
            return t[:, :].rearrange("a (p x) -> a p x", x=P)[:, :, c * CHUNK:(c + 1) * CHUNK]

        def f32(ap):
            return ap.bitcast(F32)

        def cols(src, c0, n):
            return src[0].rearrange("(k p) e -> p k e", p=P)[:, :, ds(c0, n)]

        @block.sync
        def _(sp):
            sp.dma_start(rows_a[A_NORM:A_BF2, :], attn_norm[0].rearrange("(k p) -> k p", p=P)).then_inc(rows_loaded, 16)
            sp.dma_start(rows_a[A_BF2:A_ONORM, :], gla_bf2[0].rearrange("(k p) -> k p", p=P)).then_inc(rows_loaded, 16)
            sp.dma_start(rows_a[A_ONORM:A_FNORM, :], gla_onorm[0].rearrange("(k p) -> k p", p=P)).then_inc(rows_loaded, 16)
            sp.dma_start(rows_a[A_FNORM:A_FB, :], ffn_norm[0].rearrange("(k p) -> k p", p=P)).then_inc(rows_loaded, 16)
            sp.dma_start(rows_a[A_FB:A_W2, :], ffn_conv_b[0].rearrange("(k p) -> k p", p=P)).then_inc(rows_loaded, 16)
            sp.dma_start(rows_a[A_W2:N_A, :], ffn_conv_w[0, 2].rearrange("(k p) -> k p", p=P)).then_inc(rows_loaded, 16)
            sp.dma_start(rows_b[:, :], ffn_conv_w[0, 0:2].rearrange("t (k p) -> (t k) p", p=P)).then_inc(rows_loaded, 16)
            sp.dma_start(rows_l[L_W:L_B, :], lru_conv_w[0].rearrange("t (k p) -> (t k) p", p=LT)).then_inc(rows_loaded, 16)
            for at, v in ((L_B, lru_conv_b), (L_BA, lru_ba), (L_BX, lru_bx), (L_AP, lru_a_param)):
                sp.dma_start(rows_l[at:at + LTILES, :], v[0].rearrange("(k p) -> k p", p=LT)).then_inc(rows_loaded, 16)
            sp.dma_start(wf_raw[:, :], gla_wf2[0]).then_inc(rows_loaded, 16)
            for t in range(KD):
                sp.dma_start(x_in[:, t, :], x[0, t * P:(t + 1) * P, :]).then_inc(x_loaded[t], 16)

            def load(u, src, rows=P, shape=None):
                if u.const >= 2:
                    sp.wait_ge(w_split, u.done(-1))
                    sp.sem_inc(slots_freed, 1)
                else:
                    sp.wait_ge(setup, 4)
                dst = w_raw[0:rows, u.slot(), :]
                if shape:
                    dst = dst[:, 0:shape[0] * shape[1]].rearrange("p (a b) -> p a b", b=shape[1])
                sp.dma_start(dst, src).then_inc(w_loaded[u.slot()], 16)

            def load_cols(u, w, c0, n=P):
                load(u, cols(w, c0, n), shape=(KD, n))

            load_cols(Unit(U_F), w_in, C_F)

            def load_qkv(u, h):
                load_cols(u, w_in, h * DK + C_Q)
                load_cols(u + 1, w_in, h * DK + C_K)
                load_cols(u + 2, w_in, h * DV + C_V)
                load_cols(u + 3, w_in, h * DV + (C_V + P))

            def load_g(u, h):
                load_cols(u, w_in, h * DV + C_G)
                load_cols(u + 1, w_in, h * DV + (C_G + P))

            load_qkv(Unit(U_QKV0), 0)
            with sp.Fori(0, HEADS - 1) as h:
                u = Unit(U_HEAD, 6, h)
                load_g(u, h)
                load_qkv(u + 2, h + 1)
            load_g(Unit(U_G3), HEADS - 1)
            with sp.Fori(0, KD) as c:
                u = Unit(U_YA, 2, c)
                load_cols(u, w_in, c * P + C_GA)
                load_cols(u + 1, gla_wo, c * P)

            with sp.Fori(0, LGROUPS) as g:
                for r in range(6):
                    c0 = (C_LX if r < 3 else C_LG) + (r % 3) * LT
                    load_cols(lru_unit(g, r), w_in, g * (3 * LT) + c0, LT)
                for r, wg in ((6, lru_wa), (7, lru_wx)):
                    u = lru_unit(g, r)
                    sp.wait_ge(zeroed, g * 2 + (r - 5))
                    sp.sem_inc(slots_freed, 1)
                    w = w_raw[:, u.slot(), 0:3 * 3 * LT].rearrange("p (k c) -> p k c", c=3 * LT)
                    low = wg[0, ds(g * 2, 1), :, :].rearrange("b i o -> (b i) o")
                    high = wg[0, ds(g * 2 + 1, 1), :, :].rearrange("b i o -> (b i) o")
                    cut = BW - LT
                    for dst, src in ((w[0:LT, 0, 0:BW], low[0:LT, :]), (w[0:cut, 1, 0:BW], low[LT:BW, :]),
                                     (w[cut:LT, 1, BW:2 * BW], high[0:cut, :]),
                                     (w[0:LT, 2, BW:2 * BW], high[cut:BW, :])):
                        sp.dma_start(dst, src).then_inc(w_loaded[u.slot()], 16)

            with sp.Fori(0, KD // 2) as c:
                for r in range(2):
                    load_cols(Unit(U_GB + r, 2, c), w_in, c * (2 * P) + (C_GB + r * P))
            with sp.Fori(0, KD) as c:
                for r in range(2):
                    half = lru_wo[0, r * (LW // 2):(r + 1) * (LW // 2), :]
                    load(Unit(U_YB + r, 2, c), half.rearrange("(k p) e -> p k e", p=LT)[:, :, ds(c * P, P)],
                         rows=LT, shape=(LTILES // 2, P))

            def load_rows(u0, w, nk):
                with sp.Fori(0, nk // 2) as kk:
                    for r in range(2):
                        load(Unit(u0 + r, 2, kk), w[0, ds(kk * (2 * P) + r * P, P), :])

            for half in range(2):
                load_rows(U_OUT + half * KD, w_out, KD)
            with sp.Fori(0, FT) as j:
                for r in range(2):
                    load_cols(Unit(U_UP + r, 2, j), ffn_wup, j * P + r * FF)
            for half in range(2):
                load_rows(U_DN + half * FT, ffn_wdown, FT)

        @block.gpsimd
        def _(pool):
            nc.gpsimd.memset(ident[:, :], 0.0).then_inc(setup, 1)
            nc.gpsimd.memset(causal[:, :], 1.0).then_inc(setup, 1)
            nc.gpsimd.memset(ones[:, :], 1.0).then_inc(setup, 1)
            nc.gpsimd.memset(w_raw[:, :, :], 0.0).then_inc(setup, 1)
            pool.wait_ge(setup, 4)
            nc.gpsimd.affine_select(out=ident[:, :], in_=ident[:, :], compare_op=ALU.not_equal, fill=1.0,
                                    base=0, pattern=[[-1, P]], channel_multiplier=1).then_inc(setup, 1)
            nc.gpsimd.affine_select(out=causal[:, :], in_=causal[:, :], compare_op=ALU.is_ge, fill=0.0,
                                    base=0, pattern=[[1, P]], channel_multiplier=-1).then_inc(setup, 1)
            pool.wait_ge(setup, 6)
            nc.gpsimd.memset(causal[0:CHUNK, CHUNK:P], 0.0).then_inc(setup, 1)

            with pool.Fori(0, KD) as c:
                wo = Unit(U_YA + 1, 2, c)
                pool.wait_ge(ps_free[wo.slot()], wo.ps(1))
                pool.dma_start(m_dram[:, ds(c, 1), :], m_a[:, ds(c, 1), :]).then_inc(m_stored, 16)
            with pool.Fori(0, LGROUPS) as g:
                for r in (6, 7):
                    u = lru_unit(g, r)
                    pool.wait_ge(w_split, u.done(-1))
                    pool.sem_inc(gate_slots_freed, 1)
                    nc.gpsimd.memset(w_raw[:, u.slot(), :], 0.0).then_inc(zeroed, 1)
            pool.wait_ge(m_stored, 16 * KD)
            pool.wait_ge(lru_out, LTILES)
            pool.dma_start(m[:, :, :], m_dram[:, :, :]).then_inc(m_loaded, 16)
            pool.wait_ge(m_ready, KD)
            pool.dma_start(x2[:, :, :], x[0].rearrange("(t p) d -> p t d", p=P)).then_inc(xres_loaded, 16)
            for t in range(KD):
                pool.wait_ge(acc_stored, t + 1)
                pool.dma_start(x2_dram[:, t, :], x2[:, t, :]).then_inc(x2_saved, 16)
            pool.wait_ge(x2_saved, 16 * KD)
            pool.wait_ge(unit_done, U_DN)
            pool.dma_start(y[:, :, :], x2_dram[:, :, :]).then_inc(x2_loaded, 16)
            pool.dma_start(final_gain[:, :], final_norm.partition_broadcast(P)).then_inc(x2_loaded, 16)
            for t in range(KD):
                pool.wait_ge(y_ready, t + 1)
                pool.dma_start(out[0, t * P:(t + 1) * P, :], y[:, t, :]).then_inc(out_saved, 16)
            pool.wait_ge(out_saved, 16 * KD)

        @block.scalar
        def _(act):
            order = Order(act, act_order)
            fn = nc.scalar.activation

            def round_unit(u):
                act.wait_ge(w_loaded[u.slot()], u.loaded())
                if u.const >= 2:
                    act.wait_ge(unit_done, u.done(-1))
                fn(w_hi[:, u.slot(), :], w_raw[:, u.slot(), :], ACT.Copy).then_inc(w_rounded, 1)

            def rsqrt_seed(n0, n1, nth):
                act.wait_ge(ms_ready, nth)
                order.after(fn(rs[:, n0:n1], ms[:, n0:n1], ACT.Ln))
                fn(rs[:, n0:n1], rs[:, n0:n1], ACT.Exp, scale=-0.5).then_inc(rs0_ready, 1)

            def round_transposed(dst, xr, t, nth):
                act.wait_ge(xr_ready, nth)
                fn(dst[:, :, t * P:(t + 1) * P], xr[:, t % 2, :].rearrange("p (k c) -> p k c", c=P),
                   ACT.Copy).then_inc(xr_rounded, 1)

            act.wait_ge(vecs, 3)
            fn(soft[:, 0, :], vec_l[:, L_AP:N_L], ACT.Abs).then_inc(soft_abs, 1)
            act.wait_ge(soft_abs, 1)
            fn(soft[:, 0, :], soft[:, 0, :], ACT.Exp, scale=-1.0).then_inc(soft_e, 1)
            for t in range(KD):
                act.wait_ge(x_loaded[t], 16)
                fn(h_lo[:, t, :], x_in[:, t, :], ACT.Square, accum_out=sumsq[:, t:t + 1]).then_inc(squared, 1)
                if t % 4 == 3:
                    rsqrt_seed(t - 3, t + 1, t // 4 + 1)
            round_unit(Unit(U_F))
            for t in range(KD):
                round_transposed(h_hi, xr1, t, t + 1)
            round_unit(Unit(U_QKV0))

            def gla_gate(u, h, d):
                act.wait_ge(unit_done, (u + d).done())
                fn(sg[:, d, :], pp[(u + d).slot()][:, :], ACT.Tanh, scale=0.5).then_inc(g_tanh, 1)

            def gla_qkv(u, h, final):
                round_unit(u + 1)
                act.wait_ge(z_ready, h + 1)
                fn(g1[:, :], pp[2][:, :], ACT.Abs, bias=vec_a[:, ds(h + A_BF2, 1)]).then_inc(z_abs, 1)
                act.wait_ge(z_abs, h + 1)
                order.after(fn(g1[:, :], g1[:, :], ACT.Exp, scale=-1.0))
                fn(g1[:, :], g1[:, :], ACT.Ln, bias=1.0).then_inc(sp_ready, 1)
                if final:
                    rsqrt_seed(0, PAIRS, h + 2)
                act.wait_ge(cum_ready, h + 1)
                fn(g1[:, :], cum[:, :], ACT.Exp, scale=1.0 / GATE_NORM).then_inc(gates_ready, 1)
                fn(g2[:, :], cum[:, :], ACT.Exp, scale=-1.0 / GATE_NORM).then_inc(gates_ready, 1)
                fn(decay[:, :], cum[:, CHUNK - 1:S:CHUNK], ACT.Exp, scale=1.0 / GATE_NORM)
                act.wait_ge(bdiff_ready, h + 1)
                fn(ks[:, :], ks[:, :], ACT.Exp, scale=1.0 / GATE_NORM).then_inc(gates_ready, 1)
                act.wait_ge(ps_free[u.slot()], u.ps(1))
                fn(q_chunks(q_hi, 0), chunks(g1, 0), ACT.Copy)
                fn(q_chunks(q_hi, 1), chunks(g1, 1), ACT.Copy).then_inc(qk_rounded, 1)
                round_unit(u + 2)
                act.wait_ge(ps_free[(u + 1).slot()], (u + 1).ps(1))
                fn(k_hi[:, :], g2[:, :], ACT.Copy).then_inc(qk_rounded, 1)
                round_unit(u + 3)
                for d in range(2):
                    v = u + (2 + d)
                    act.wait_ge(unit_done, v.done())
                    if d == 0 and final:
                        act.wait_ge(oT_ready, h * 2)
                    fn(vo[:, :, d * P:(d + 1) * P], pp[v.slot()][:, :].rearrange("p (n c) -> p n c", c=P),
                       ACT.Copy).then_inc(ps_free[v.slot()], 1)
                    if d == 0:
                        round_unit(u + 4)

            def gla_steps(u, h):
                def round_kv(p):
                    act.wait_ge(tr_ready, h * PAIRS + (p + 1))
                    fn(kt_hi[0:CHUNK, 0, :], tr_ps[0:CHUNK, 0:P], ACT.Copy)
                    fn(kt_hi[CHUNK:P, 1, :], tr_ps[CHUNK:P, 0:P], ACT.Copy)
                    fn(v_hi[:, p % 2, :], tr_ps[:, P:], ACT.Copy).then_inc(kv_rounded, 1)

                round_kv(0)
                for p in range(PAIRS):
                    n = h * PAIRS + p
                    act.wait_ge(at_masked, n + 1)
                    fn(at_hi[:, :], at_raw[:, :], ACT.Copy).then_inc(at_rounded, 1)
                    act.wait_ge(s_updated, n * 2 + 1)
                    fn(s_hi[:, 1, :], s_raw[:, :], ACT.Copy).then_inc(s_rounded, 1)
                    if p + 1 < PAIRS:
                        round_kv(p + 1)
                    if p % 4 == 0:
                        round_unit(u + (1 + p // 4))
                    if p == 5:
                        gla_gate(u, h, 0)
                    act.wait_ge(o_ready, n + 1)
                    order.after(fn(vo[:, p, :], o_ps, ACT.Copy))
                    fn(squares[:, :], vo[:, p, :], ACT.Square, accum_out=sumsq[:, p:p + 1]).then_inc(o_stored, 1)
                    act.wait_ge(s_updated, n * 2 + 2)
                    fn(s_hi[:, 0, :], s_raw[:, :], ACT.Copy).then_inc(s_rounded, 1)
                gla_gate(u, h, 1)

            gla_qkv(Unit(U_QKV0), 0, False)
            with act.Fori(0, HEADS - 1) as h:
                order.enter(h, PAIRS + 2)
                gla_steps(Unit(U_HEAD, 6, h), h)
                gla_qkv(Unit(U_HEAD + 2, 6, h), h + 1, True)
            order.leave(HEADS - 1)
            gla_steps(Unit(U_G3), HEADS - 1)
            rsqrt_seed(0, PAIRS, 2 + HEADS)

            round_unit(Unit(U_YA + 1))
            for k in range(2 * HEADS):
                if k == 2 * (HEADS - 1):
                    act.wait_ge(og_ready, 2 * HEADS)
                fn(og_hi[:, k, :], og_raw[:, k, :], ACT.Copy).then_inc(og_rounded, 1)
            with act.Fori(0, KD) as c:
                u = Unit(U_YA, 2, c)
                act.wait_ge(unit_done, u.done())
                act.wait_ge(ps_free[(u + 1).slot()], (u + 1).ps())
                fn(t_a[:, :], pp[u.slot()][:, :], ACT.Tanh, scale=0.5).then_inc(ps_free[u.slot()], 1)
                round_unit(u + 2)
                round_unit(u + 3)

            act.wait_ge(m_stored, 16 * KD)

            def decay_terms(g, o):
                scale, minus = sp2[:, ds(g * 3 + o, 1)], minus_sp4[:, ds(g * 3 + o, 1)]
                order.after(fn(lw[:, o, :], la[:, o, :], ACT.Exp, scale=minus, bias=minus))
                order.after(fn(la[:, o, :], la[:, o, :], ACT.Tanh, scale=scale, bias=scale))

            def root(o):
                fn(la[:, o, :], la[:, o, :], ACT.Sqrt).then_inc(lru_act, 1)

            def decay_of(g, u):
                round_unit(u + 1)
                decay_terms(g, 0)
                root(0)
                decay_terms(g, 1)
                decay_terms(g, 2)
                round_unit(u + 2)
                root(1)
                root(2)

            def gelu_gate(g, o):
                u = lru_unit(g, 3 + o)
                act.wait_ge(unit_done, u.done())
                fn(hl[:, ds(g * 3 + o, 1), :].rearrange("p a s -> p (a s)"),
                   pp[u.slot()][0:LT, :], ACT.Gelu_apprx_tanh).then_inc(ps_free[u.slot()], 1)

            def lru_group(g):
                for r in range(2, 7):
                    round_unit(lru_unit(g, r + 1))
                    if r >= 4:
                        gelu_gate(g, r - 4)
                for o in range(3):
                    u = lru_unit(g, 6)
                    if o == 2:
                        act.wait_ge(unit_done, u.done())
                        round_unit(lru_unit(g, 8))
                    else:
                        act.wait_ge(ra_ready, g * 2 + (o + 1))
                    fn(la[:, o, :], pp[2][0:LT, :], ACT.Tanh, scale=0.5,
                       bias=half_b[:, ds(g * 3 + o, 1)]).then_inc(ra_free, 1)
                    act.wait_ge(rx_ready, g * 3 + (o + 1))
                    fn(lc[:, o, :], pp[3][0:LT, :], ACT.Tanh, scale=0.5,
                       bias=half_b[:, ds(g * 3 + (o + LTILES), 1)]).then_inc(rx_free, 1)

            round_unit(lru_unit(0, 2))
            lru_group(0)
            with act.Fori(1, LGROUPS) as g:
                order.enter(g - 1, 3 * 2)
                decay_of(g - 1, lru_unit(g, 0))
                lru_group(g)
            order.leave(LGROUPS - 1)

            def merge_gate(u, c):
                act.wait_ge(unit_done, u.done())
                fn(t_b[:, ds(c, 1), :].rearrange("p a s -> p (a s)"), pp[u.slot()][:, :],
                   ACT.Tanh, scale=0.5).then_inc(ps_free[u.slot()], 1)

            decay_of(LGROUPS - 1, late_unit(U_GB))
            act.wait_ge(gated, LTILES)
            merge_gate(late_unit(U_GB), 0)
            merge_gate(late_unit(U_GB + 1), 1)
            act.wait_ge(lru_out, LTILES)
            with act.Fori(1, KD // 2) as c:
                for r in range(2):
                    u = late_unit(U_GB + r, 2, c)
                    round_unit(u + 1)
                    merge_gate(u, c * 2 + r)
            act.wait_ge(unit_done, U_YB)
            for k in range(LTILES):
                fn(hl_hi[:, k, :], hl[:, k, :], ACT.Copy).then_inc(hl_rounded, 1)
                if k == 3:
                    round_unit(late_unit(U_YB + 1))
            for r in range(1, 4):
                round_unit(late_unit(U_YB + r + 1))
            with act.Fori(1, KD // 2) as c:
                for r in range(4):
                    round_unit(late_unit(U_YB + r + 1, 4, c))

            def contract(raw, a_hi, nk, u0, scale, ready, nth, last):
                for half in range(2):
                    def step(kk, r, more=True):
                        k = kk * 2 + r
                        u = late_unit(u0 + half * nk + r, 2, kk) if not isinstance(kk, int) else \
                            late_unit(u0 + half * nk + 2 * kk + r)
                        if half == 0:
                            act.wait_ge(ready, k + 1)
                        act.wait_ge(unit_done, u.done(-1))
                        fn(a_hi[:, u.slot(), :], raw[:, ds(k, 1), half * HALF:(half + 1) * HALF].rearrange(
                            "p a s -> p (a s)"), ACT.Copy, scale=scale).then_inc(a_rounded, 1)
                        if more:
                            round_unit(u + 1)
                    end = nk // 2 - (1 if last and half else 0)
                    with act.Fori(0, end) as kk:
                        step(kk, 0)
                        step(kk, 1)
                    if last and half:
                        step(end, 0)
                        step(end, 1, more=False)

            contract(m, ao_hi, KD, U_OUT, 0.5, m_ready, 0, False)
            for t in range(KD):
                act.wait_ge(acc_stored, t + 1)
                act.wait_ge(squared, KD + t)
                fn(yb[:, :], x2[:, t, :], ACT.Square, accum_out=sumsq[:, t:t + 1]).then_inc(squared, 1)
                if t % 4 == 3:
                    rsqrt_seed(t - 3, t + 1, 2 + HEADS + t // 4 + 1)
            for t in range(KD):
                round_transposed(g_hi, xr2, t, KD + t + 1)

            act.wait_ge(x2_saved, 16 * KD)

            def ffn_tile(j):
                u = ffn_unit(j)
                round_unit(u + 1)
                act.wait_ge(unit_done, u.done())
                if not isinstance(j, int):
                    act.wait_ge(hid_ready, j)
                fn(ug[:, :], pp[u.slot()][:, :], ACT.Identity, scale=vec_a[:, ds(j + A_W2, 1)],
                   bias=vec_a[:, ds(j + A_FB, 1)]).then_inc(u_first, 1)
                round_unit(u + 2)
                act.wait_ge(ps_free[u.slot()], u.ps(1))
                fn(ug[:, :], ug[:, :], ACT.Gelu_apprx_tanh).then_inc(u_gelu, 1)
                v = u + 1
                act.wait_ge(unit_done, v.done())
                fn(uv[:, :], pp[v.slot()][:, :], ACT.Identity, scale=vec_a[:, ds(j + (A_W2 + FT), 1)],
                   bias=vec_a[:, ds(j + (A_FB + FT), 1)]).then_inc(u_first, 1)

            ffn_tile(0)
            with act.Fori(1, FT) as j:
                ffn_tile(j)
            contract(hid, ad_hi, FT, U_DN, 1.0, hid_ready, 2 * KD, True)

            for t in range(KD):
                act.wait_ge(acc_stored, KD + t + 1)
                act.wait_ge(squared, 2 * KD + t)
                fn(junk[:, :], y[:, t, :], ACT.Square, accum_out=sumsq[:, t:t + 1]).then_inc(squared, 1)
                if t % 4 == 3:
                    rsqrt_seed(t - 3, t + 1, 4 + HEADS + t // 4 + 1)

        @block.vector
        def _(dve):
            order = Order(dve, dve_order)
            after = order.after
            ts, tt, stt = nc.vector.tensor_scalar, nc.vector.tensor_tensor, nc.vector.scalar_tensor_tensor
            copy = nc.vector.tensor_copy

            def split_unit(u):
                dve.wait_ge(w_rounded, u.done())
                tt(w_lo[:, u.slot(), :], w_raw[:, u.slot(), :], f32(w_hi[:, u.slot(), :]),
                   ALU.subtract).then_inc(w_split, 1)

            def rsqrt(n0, n1, width, sums, nth):
                dve.wait_ge(*sums)
                ts(ms[:, n0:n1], sumsq[:, n0:n1], 1.0 / width, EPS, ALU.mult, ALU.add).then_inc(ms_ready, 1)
                dve.wait_ge(ms_ready, nth)
                dve.wait_ge(rs0_ready, nth)
                after(tt(newton[:, n0:n1], rs[:, n0:n1], rs[:, n0:n1], ALU.mult))
                after(tt(newton[:, n0:n1], newton[:, n0:n1], ms[:, n0:n1], ALU.mult))
                after(ts(newton[:, n0:n1], newton[:, n0:n1], -0.5, 1.5, ALU.mult, ALU.add))
                after(tt(rs[:, n0:n1], rs[:, n0:n1], newton[:, n0:n1], ALU.mult))

            def norm_transposed(src, xn, xr, gain0, dst_hi, dst_lo, base):
                gain = vec_a[:, gain0:gain0 + KD].unsqueeze(2).broadcast_to([P, KD, P])

                def scale(t):
                    if t >= 2:
                        dve.wait_ge(xT_ready, base + t - 1)
                    ts(xn[:, t % 2, :], src[:, t, :], rs[:, t:t + 1], None, ALU.mult).then_inc(xn_ready, 1)

                scale(0)
                scale(1)
                for t in range(KD):
                    dve.wait_ge(xT_ready, base + t + 1)
                    tt(xr[:, t % 2, :].rearrange("p (k c) -> p k c", c=P),
                       pp[t % 4][:, :].rearrange("p (k c) -> p k c", c=P), gain, ALU.mult).then_inc(xr_ready, 1)
                    if t + 2 < KD:
                        scale(t + 2)
                    dve.wait_ge(xr_ready, base + t + 1)
                    dve.wait_ge(xr_rounded, base + t + 1)
                    tt(dst_lo[:, :, t * P:(t + 1) * P], xr[:, t % 2, :].rearrange("p (k c) -> p k c", c=P),
                       f32(dst_hi[:, :, t * P:(t + 1) * P]), ALU.subtract).then_inc(xT_split, 1)
                dve.wait_ge(xT_split, base + KD)

            dve.wait_ge(vecs_T, 3)
            copy(vec_a[:, :], pp[0][:, 0:N_A]).then_inc(vecs, 1)
            copy(vec_b[:, :], pp[1][:, 0:N_B]).then_inc(vecs, 1)
            copy(vec_l[:, :], pp[2][0:LT, 0:N_L]).then_inc(vecs, 1)
            dve.wait_ge(vecs, 3)
            ts(onorm_half[:, :], vec_a[:, A_ONORM:A_FNORM], 0.5, None, ALU.mult)
            ts(half_b[:, :], vec_l[:, L_BA:L_AP], 0.5, None, ALU.mult)
            e, s, z, poly = (soft[:, n, :] for n in range(4))
            dve.wait_ge(soft_e, 1)
            after(ts(s, e, 2.0, None, ALU.add))
            after(nc.vector.reciprocal(s, s))
            after(tt(s, s, e, ALU.mult))
            after(tt(z, s, s, ALU.mult))
            after(ts(poly, z, 1.0 / 17, 1.0 / 15, ALU.mult, ALU.add))
            for n in (13, 11, 9, 7, 5, 3, 1):
                after(tt(poly, poly, z, ALU.mult))
                after(ts(poly, poly, 1.0 / n, None, ALU.add))
            after(tt(poly, poly, s, ALU.mult))
            after(ts(z, vec_l[:, L_AP:N_L], 0.0, 2.0, ALU.max, ALU.mult))
            after(stt(sp2[:, :], poly, 4.0, z, ALU.mult, ALU.add))
            ts(minus_sp4[:, :], sp2[:, :], -2.0, None, ALU.mult)

            rsqrt(0, 4, D, (squared, 4), 1)
            rsqrt(4, 8, D, (squared, 8), 2)
            norm_transposed(x_in, xn1, xr1, A_NORM, h_hi, h_lo, 0)
            split_unit(Unit(U_F))
            for t in (q_hi, q_lo):
                nc.vector.memset(f32(t[:, :]), 0.0)
            for t in (kt_hi, kt_lo):
                nc.vector.memset(f32(t[:, :, :]), 0.0)
            split_unit(Unit(U_QKV0))

            dve.wait_ge(rows_loaded, 16 * 13)
            dve.wait_ge(unit_done, 1)
            after(copy(f_hi[:, :], pp[0][0:RANK, :]))
            tt(f_lo[:, :], pp[0][0:RANK, :], f32(f_hi[:, :]), ALU.subtract).then_inc(ps_free[0], 1)

            def forget_weights(h):
                part = wf_raw[:, ds(h * DK, DK)]
                after(copy(wf_hi[:, :], part))
                tt(wf_lo[:, :], part, f32(wf_hi[:, :]), ALU.subtract).then_inc(wf_ready, 1)

            def gla_qkv(u, h, final):
                bias = vec_a[:, ds(h + A_BF2, 1)]
                split_unit(u + 1)
                dve.wait_ge(z_abs, h + 1)
                ts(cum[:, :], pp[2][:, :], bias, 0.0, ALU.add, ALU.min).then_inc(z_free, 1)
                dve.wait_ge(z_free, h + 1)
                dve.wait_ge(sp_ready, h + 1)
                after(tt(cum[:, :], cum[:, :], g1[:, :], ALU.subtract))
                for n in range(S // CHUNK):
                    part = cum[:, n * CHUNK:(n + 1) * CHUNK]
                    scan = nc.vector.tensor_tensor_scan(part, ones[:, :], part, 0.0, ALU.mult, ALU.add)
                scan.then_inc(cum_ready, 1)
                dve.wait_ge(cum_ready, h + 1)
                by_chunk = cum[:, :].rearrange("p (n c) -> p n c", c=CHUNK)
                tt(ks[:, :].rearrange("p (n c) -> p n c", c=CHUNK),
                   by_chunk[:, :, CHUNK - 1:CHUNK].broadcast_to([P, S // CHUNK, CHUNK]), by_chunk,
                   ALU.subtract).then_inc(bdiff_ready, 1)
                if final:
                    rsqrt(0, PAIRS, DV, (o_stored, h * PAIRS), h + 2)
                    tt(vo[:, :, :], vo[:, :, :], rs[:, :].unsqueeze(2).broadcast_to([P, PAIRS, DV]),
                       ALU.mult).then_inc(on_ready, 1)
                dve.wait_ge(gates_ready, h * 3 + 1)
                dve.wait_ge(unit_done, u.done())
                stt(g1[:, :], pp[u.slot()][:, :], DK ** -0.5, g1[:, :], ALU.mult, ALU.mult).then_inc(ps_free[u.slot()], 1)
                dve.wait_ge(qk_rounded, h * 2 + 1)
                for c in range(2):
                    tt(q_chunks(q_lo, c), chunks(g1, c), f32(q_chunks(q_hi, c)), ALU.subtract)
                split_unit(u + 2)
                k = u + 1
                dve.wait_ge(gates_ready, h * 3 + 3)
                dve.wait_ge(unit_done, k.done())
                tt(g2[:, :], pp[k.slot()][:, :], g2[:, :], ALU.mult)
                tt(ks[:, :], pp[k.slot()][:, :], ks[:, :], ALU.mult).then_inc(ps_free[k.slot()], 1)
                dve.wait_ge(qk_rounded, h * 2 + 2)
                tt(k_lo[:, :], g2[:, :], f32(k_hi[:, :]), ALU.subtract).then_inc(qk_split, 1)
                split_unit(u + 3)
                if final:
                    gla_final(h - 1)
                split_unit(u + 4)

            def gla_final(h):
                for d, ps in ((0, pp[3]), (1, pp[2])):
                    dve.wait_ge(oT_ready, h * 2 + (d + 1))
                    stt(og_raw[:, ds(h * 2 + d, 1), :].rearrange("p a s -> p (a s)"), ps[:, :],
                        onorm_half[:, d:d + 1], sg[:, d, :], ALU.mult, ALU.mult).then_inc(og_ready, 1)

            def gla_gate(u, h, d):
                dve.wait_ge(g_tanh, h * 2 + (d + 1))
                stt(sg[:, d, :], sg[:, d, :], 1.0, pp[(u + d).slot()][:, :], ALU.add,
                    ALU.mult).then_inc(ps_free[(u + d).slot()], 1)

            def gla_steps(u, h, more=True):
                nc.vector.memset(s_raw[:, :], 0.0)
                nc.vector.memset(f32(s_hi[:, 0, :]), 0.0)
                nc.vector.memset(f32(s_lo[:, 0, :]), 0.0).then_inc(s_cleared, 1)
                dve.wait_ge(s_cleared, h + 1)

                def split_kv(p):
                    dve.wait_ge(kv_rounded, h * PAIRS + (p + 1))
                    for c in range(2):
                        rows = slice(c * CHUNK, (c + 1) * CHUNK)
                        tt(kt_lo[rows, c, :], tr_ps[rows, 0:P], f32(kt_hi[rows, c, :]), ALU.subtract)
                    if p == 0:
                        dve.wait_ge(at_ready, h * PAIRS + 1)
                    tt(v_lo[:, p % 2, :], tr_ps[:, P:], f32(v_hi[:, p % 2, :]), ALU.subtract).then_inc(kv_split, 1)

                split_kv(0)
                for p in range(PAIRS):
                    n = h * PAIRS + p
                    nc.vector.copy_predicated(at_raw[:, :], causal[:, :].bitcast(mybir.dt.uint32),
                                              at_ps).then_inc(at_masked, 1)
                    dve.wait_ge(at_rounded, n + 1)
                    tt(at_lo[:, :], at_raw[:, :], f32(at_hi[:, :]), ALU.subtract).then_inc(at_split, 1)
                    dve.wait_ge(ds_ready, n + 1)
                    for c in range(2):
                        slot = 1 - c
                        stt(s_raw[:, :], s_raw[:, :], decay[:, 2 * p + c:2 * p + c + 1],
                            ds_ps[:, c * DV:(c + 1) * DV], ALU.mult, ALU.add).then_inc(s_updated, 1)
                        if c:
                            if p + 1 < PAIRS:
                                split_kv(p + 1)
                            if p % 4 == 0:
                                split_unit(u + (1 + p // 4))
                            if p == 5:
                                gla_gate(u, h, 0)
                            if p == 6 and more:
                                forget_weights(h + 1)
                            if p + 1 < PAIRS:
                                dve.wait_ge(at_ready, n + 2)
                        dve.wait_ge(s_updated, n * 2 + (c + 1))
                        dve.wait_ge(s_rounded, n * 2 + (c + 1))
                        tt(s_lo[:, slot, :], s_raw[:, :], f32(s_hi[:, slot, :]), ALU.subtract).then_inc(s_split, 1)
                gla_gate(u, h, 1)

            nc.vector.memset(at_raw[:, :], 0.0)
            forget_weights(0)
            gla_qkv(Unit(U_QKV0), 0, False)
            with dve.Fori(0, HEADS - 1) as h:
                order.enter(h, 1 + 1 + 4)
                gla_steps(Unit(U_HEAD, 6, h), h)
                gla_qkv(Unit(U_HEAD + 2, 6, h), h + 1, True)
            order.leave(HEADS - 1)
            gla_steps(Unit(U_G3), HEADS - 1, more=False)
            rsqrt(0, PAIRS, DV, (o_stored, HEADS * PAIRS), 2 + HEADS)
            tt(vo[:, :, :], vo[:, :, :], rs[:, :].unsqueeze(2).broadcast_to([P, PAIRS, DV]),
               ALU.mult).then_inc(on_ready, 1)

            split_unit(Unit(U_YA + 1))
            for k in range(2 * HEADS):
                if k == 2 * (HEADS - 1):
                    gla_final(HEADS - 1)
                    dve.wait_ge(og_ready, 2 * HEADS)
                dve.wait_ge(og_rounded, k + 1)
                tt(og_lo[:, k, :], og_raw[:, k, :], f32(og_hi[:, k, :]), ALU.subtract).then_inc(og_split, 1)
            with dve.Fori(0, KD) as c:
                u = Unit(U_YA, 2, c)
                wo = u + 1
                split_unit(u + 2)
                split_unit(u + 3)
                dve.wait_ge(ps_free[u.slot()], u.ps(1))
                dve.wait_ge(unit_done, wo.done())
                stt(m_a[:, ds(c, 1), :].rearrange("p a s -> p (a s)"), t_a[:, :], 1.0,
                    pp[wo.slot()][:, :], ALU.add, ALU.mult).then_inc(ps_free[wo.slot()], 1)

            dve.wait_ge(m_stored, 16 * KD)

            def convolve(g, r):
                u = lru_unit(g, r)
                ps = pp[u.slot()]

                def col(at):
                    return vec_l[:, ds(g * 3 + (at + r), 1)]

                dve.wait_ge(unit_done, u.done())
                if r:
                    dve.wait_ge(xc_split, g * 3 + r)
                after(ts(conv[:, :], ps[0:LT, :], col(L_W + 3 * LTILES), col(L_B), ALU.mult, ALU.add))
                after(stt(conv[:, 1:], ps[0:LT, :S - 1], col(L_W + 2 * LTILES), conv[:, 1:], ALU.mult, ALU.add))
                after(stt(conv[:, 2:], ps[0:LT, :S - 2], col(L_W + LTILES), conv[:, 2:], ALU.mult, ALU.add))
                stt(conv[:, 3:], ps[0:LT, :S - 3], col(L_W), conv[:, 3:], ALU.mult,
                    ALU.add).then_inc(ps_free[u.slot()], 1)
                dve.wait_ge(ps_free[u.slot()], u.ps(1))
                after(copy(xc_hi[:, r, :], conv[:, :]))
                tt(xc_lo[:, r, :], conv[:, :], f32(xc_hi[:, r, :]), ALU.subtract).then_inc(xc_split, 1)

            def gated_input(g, o):
                C = lc[:, o, :]
                dve.wait_ge(rx_free, g * 3 + (o + 1))
                after(tt(conv[:, :], f32(xc_hi[:, o, :]), f32(xc_lo[:, o, :]), ALU.add))
                stt(C, C, 1.0, conv[:, :], ALU.add, ALU.mult).then_inc(gated, 1)
                dve.wait_ge(gated, g * 3 + (o + 1))

            def recur(g, o):
                A, B, C = lw[:, o, :], la[:, o, :], lc[:, o, :]
                gate = lru_unit(g, 3 + o)
                dve.wait_ge(lru_act, g * 3 + (o + 1))
                after(stt(B, A, 1.0, B, ALU.add, ALU.mult))
                after(stt(B, B, 0.5, C, ALU.mult, ALU.mult))
                after(nc.vector.tensor_tensor_scan(C, A, B, 0.0, ALU.mult, ALU.add))
                dve.wait_ge(ps_free[gate.slot()], gate.ps(1))
                out_tile = hl[:, ds(g * 3 + o, 1), :].rearrange("p a s -> p (a s)")
                tt(out_tile, out_tile, C, ALU.mult).then_inc(lru_out, 1)

            def lru_group(g, before):
                before(0)
                for r in range(3):
                    split_unit(lru_unit(g, r + 2))
                    convolve(g, r)
                for r in (5, 6):
                    split_unit(lru_unit(g, r))
                    before(r - 4)
                split_unit(lru_unit(g, 7))
                gated_input(g, 0)
                gated_input(g, 1)
                split_unit(lru_unit(g, 8))
                gated_input(g, 2)

            lru_group(0, lambda o: None)
            with dve.Fori(1, LGROUPS) as g:
                order.enter(g - 1, 3 * 4 + 3 + 3 * 3)
                split_unit(lru_unit(g, 1))
                lru_group(g, lambda o: recur(g - 1, o))
            order.leave(LGROUPS - 1)
            for o in range(3):
                if o < 2:
                    split_unit(late_unit(U_GB + o + 1))
                recur(LGROUPS - 1, o)

            for n in range(2, KD):
                split_unit(late_unit(U_GB + n + 1))
            for k in range(LTILES):
                dve.wait_ge(hl_rounded, k + 1)
                tt(hl_lo[:, k, :], hl[:, k, :], f32(hl_hi[:, k, :]), ALU.subtract).then_inc(hl_split, 1)
                if k == 3:
                    split_unit(late_unit(U_YB + 1))

            def branch_b(i, n, u):
                c = i * 2 + n
                dve.wait_ge(unit_done, u.done())
                stt(yb[:, :], t_b[:, ds(c, 1), :].rearrange("p a s -> p (a s)"), 1.0, pp[2 + n][:, :],
                    ALU.add, ALU.mult).then_inc(yb_free[n], 1)
                dve.wait_ge(yb_free[n], i + 1)
                merged = m[:, ds(c, 1), :].rearrange("p a s -> p (a s)")
                tt(merged, merged, yb[:, :], ALU.add).then_inc(m_ready, 1)
                dve.wait_ge(m_ready, c + 1)

            dve.wait_ge(m_loaded, 16)
            for r in range(1, 4):
                split_unit(late_unit(U_YB + r + 1))
                if r == 1:
                    branch_b(0, 0, late_unit(U_YB + 1))
            branch_b(0, 1, late_unit(U_YB + 3))
            with dve.Fori(1, KD // 2) as c:
                u = late_unit(U_YB, 4, c)
                for n in range(2):
                    split_unit(u + (2 * n + 1))
                    split_unit(u + (2 * n + 2))
                    branch_b(c, n, u + (2 * n + 1))

            def contract(raw, a_hi, a_lo, nk, u0, scale, nth, last, residual, stored):
                for half in range(2):
                    def split_act(kk, r):
                        k = kk * 2 + r
                        slot = (u0 + r) % 2
                        dve.wait_ge(a_rounded, k + (nth + half * nk + 1))
                        stt(a_lo[:, slot, :], raw[:, ds(k, 1), half * HALF:(half + 1) * HALF].rearrange(
                            "p a s -> p (a s)"), scale, f32(a_hi[:, slot, :]), ALU.mult,
                            ALU.subtract).then_inc(a_split, 1)

                    def unit(kk, r):
                        return late_unit(u0 + half * nk + 2 * kk + r) if isinstance(kk, int) else \
                            late_unit(u0 + half * nk + r, 2, kk)

                    def store(t0):
                        for t in range(4):
                            dve.wait_ge(unit_done, u0 + (t0 // 4 + 1) * nk)
                            tt(residual[:, t0 + t, :], pp[t][:, :], residual[:, t0 + t, :],
                               ALU.add).then_inc(acc_stored, 1)

                    split_act(0, 0)
                    if half:
                        store(0)
                    split_unit(unit(0, 1))
                    split_act(0, 1)
                    split_unit(unit(0, 2))
                    end = nk // 2 - (1 if last and half else 0)
                    with dve.Fori(1, end) as kk:
                        for r in range(2):
                            split_act(kk, r)
                            split_unit(unit(kk, r + 1))
                    if last and half:
                        split_act(end, 0)
                        split_unit(unit(end, 1))
                        split_act(end, 1)
                    if not half:
                        dve.wait_ge(*stored)
                store(4)
                dve.wait_ge(acc_stored, nth // (2 * KD) * KD + KD)

            contract(m, ao_hi, ao_lo, KD, U_OUT, 0.5, 0, False, x2, (xres_loaded, 16))
            rsqrt(0, 4, D, (squared, KD + 4), 3 + HEADS)
            rsqrt(4, 8, D, (squared, KD + 8), 4 + HEADS)
            norm_transposed(x2, xn2, xr2, A_FNORM, g_hi, g_lo, KD)

            dve.wait_ge(x2_saved, 16 * KD)
            with dve.Fori(0, FT) as j:
                order.enter(j, 2)
                u = late_unit(U_UP, 2, j, apart=LGROUPS + 2 * KD)
                for n, acc in ((0, ug), (1, uv)):
                    split_unit(u + (n + 1))
                    ps = pp[(u + n).slot()]
                    dve.wait_ge(u_first, j * 2 + (n + 1))
                    after(stt(acc[:, 1:], ps[:, :S - 1], vec_b[:, ds(j + (2 + n) * FT, 1)], acc[:, 1:],
                              ALU.mult, ALU.add))
                    stt(acc[:, 2:], ps[:, :S - 2], vec_b[:, ds(j + n * FT, 1)], acc[:, 2:],
                        ALU.mult, ALU.add).then_inc(ps_free[(u + n).slot()], 1)
                dve.wait_ge(ps_free[(u + 1).slot()], (u + 1).ps(1))
                dve.wait_ge(u_gelu, j + 1)
                tt(hid[:, ds(j, 1), :].rearrange("p a s -> p (a s)"), ug[:, :], uv[:, :],
                   ALU.mult).then_inc(hid_ready, 1)
            order.leave(FT)
            contract(hid, ad_hi, ad_lo, FT, U_DN, 1.0, 2 * KD, True, y, (x2_loaded, 32))

            for q in range(2):
                rsqrt(4 * q, 4 * q + 4, D, (squared, 2 * KD + 4 * q + 4), 5 + HEADS + q)
                for t in range(4 * q, 4 * q + 4):
                    stt(y[:, t, :], y[:, t, :], rs[:, t:t + 1], final_gain[:, :], ALU.mult,
                        ALU.mult).then_inc(y_ready, 1)

        @block.tensor
        def _(pe):
            mm = nc.tensor.matmul

            def split_product(dst, s_hi_, s_lo_, m_hi_, m_lo_, start, stop):
                mm(dst, s_hi_, m_hi_, start=start, stop=False)
                mm(dst, s_hi_, m_lo_, start=False, stop=False)
                return mm(dst, s_lo_, m_hi_, start=False, stop=stop)

            def weights(u, k, n=P, rows=P):
                return (w_hi[0:rows, u.slot(), k * n:(k + 1) * n], w_lo[0:rows, u.slot(), k * n:(k + 1) * n])

            def begin(u):
                pe.wait_ge(w_split, u.done())
                if not (u.i is None and u.ps() == 0):
                    pe.wait_ge(ps_free[u.slot()], u.ps())

            def project(u, a_hi, a_lo, n=P, parts=range(8), wait_k=None):
                if 0 in parts:
                    begin(u)
                for part in parts:
                    half, k0 = part // 4, 2 * (part % 4)
                    for k in (k0, k0 + 1):
                        if wait_k and half == 0:
                            pe.wait_ge(wait_k, k + 1)
                        tok = slice(half * HALF, (half + 1) * HALF)
                        last = split_product(pp[u.slot()][0:n, tok], *weights(u, k, n), a_hi[:, k, tok],
                                             a_lo[:, k, tok], k == 0, k == KD - 1)
                if 7 in parts:
                    last.then_inc(unit_done, 1)

            def transpose_tiles(xn, base, free):
                for t in range(KD):
                    pe.wait_ge(xn_ready, base + t + 1)
                    if t >= 4:
                        pe.wait_ge(xr_ready, base + t - 3)
                    elif free:
                        pe.wait_ge(*free)
                    for k in range(KD):
                        last = nc.tensor.transpose(pp[t % 4][:, k * P:(k + 1) * P],
                                                   xn[:, t % 2, k * P:(k + 1) * P], ident[:, :])
                    last.then_inc(xT_ready, 1)

            pe.wait_ge(setup, 7)
            pe.wait_ge(rows_loaded, 16 * 13)
            nc.tensor.transpose(pp[0][:, 0:N_A], rows_a[:, :], ident[0:N_A, 0:N_A]).then_inc(vecs_T, 1)
            nc.tensor.transpose(pp[1][:, 0:N_B], rows_b[:, :], ident[0:N_B, 0:N_B]).then_inc(vecs_T, 1)
            nc.tensor.transpose(pp[2][0:LT, 0:N_L], rows_l[:, :], ident[0:N_L, 0:N_L]).then_inc(vecs_T, 1)
            transpose_tiles(xn1, 0, (vecs, 3))
            pe.wait_ge(xT_split, KD)
            project(Unit(U_F), h_hi, h_lo)

            def gla_qkv(u, h, final):
                project(u, h_hi, h_lo, parts=range(2))
                pe.wait_ge(wf_ready, h + 1)
                if final:
                    pe.wait_ge(o_stored, h * PAIRS)
                else:
                    pe.wait_ge(ps_free[0], 1)
                for half in range(2):
                    tok = slice(half * HALF, (half + 1) * HALF)
                    last = split_product(pp[2][:, tok], wf_hi[:, :], wf_lo[:, :], f_hi[:, tok], f_lo[:, tok],
                                         True, True)
                last.then_inc(z_ready, 1)
                project(u, h_hi, h_lo, parts=range(2, 8))
                project(u + 1, h_hi, h_lo)
                if final:
                    gla_final(h - 1)
                project(u + 2, h_hi, h_lo)
                project(u + 3, h_hi, h_lo)

            def gla_final(h):
                pe.wait_ge(on_ready, h + 1)
                pe.wait_ge(s_updated, (h + 1) * (2 * PAIRS))
                for d, ps in ((0, pp[3]), (1, pp[2])):
                    for p in range(PAIRS):
                        last = nc.tensor.transpose(ps[:, p * P:(p + 1) * P], vo[:, p, d * P:(d + 1) * P], ident[:, :])
                    last.then_inc(oT_ready, 1)

            def gla_steps(u, h):
                def gate_part(i):
                    project(u + i // 8, h_hi, h_lo, parts=[i % 8])

                def transpose_kv(p):
                    tok = slice(p * P, (p + 1) * P)
                    nc.tensor.transpose(tr_ps[:, 0:P], ks[:, tok], ident[:, :])
                    nc.tensor.transpose(tr_ps[:, P:2 * P], vo[:, p, 0:P], ident[:, :])
                    nc.tensor.transpose(tr_ps[:, 2 * P:], vo[:, p, P:], ident[:, :]).then_inc(tr_ready, 1)

                gate_part(0)
                pe.wait_ge(qk_split, h + 1)
                for v in (0, 1):
                    w = u + (v - 2)
                    pe.wait_ge(ps_free[w.slot()], w.ps(1))
                pe.wait_ge(z_free, h + 1)
                transpose_kv(0)
                for p in range(PAIRS):
                    n = h * PAIRS + p
                    tok = slice(p * P, (p + 1) * P)
                    if p:
                        pe.wait_ge(at_masked, n)
                    split_product(at_ps, k_hi[:, tok], k_lo[:, tok], gla_q_tokens(q_hi, p), gla_q_tokens(q_lo, p),
                                  True, True).then_inc(at_ready, 1)
                    if p + 1 < PAIRS:
                        gate_part(2 * p + 1)
                    pe.wait_ge(kv_split, n + 1)
                    if p:
                        pe.wait_ge(s_updated, n * 2)
                    for c in range(2):
                        last = split_product(ds_ps[:, c * DV:(c + 1) * DV], kt_hi[:, c, :], kt_lo[:, c, :],
                                             v_hi[:, p % 2, :], v_lo[:, p % 2, :], True, True)
                    last.then_inc(ds_ready, 1)
                    if p + 1 < PAIRS:
                        transpose_kv(p + 1)
                    gate_part(min(2 * p + 2, 2 * PAIRS - 1))
                    if p:
                        pe.wait_ge(o_stored, n)
                    pe.wait_ge(at_split, n + 1)
                    split_product(o_ps, at_hi[:, :], at_lo[:, :], v_hi[:, p % 2, :], v_lo[:, p % 2, :], True, False)
                    if p:
                        pe.wait_ge(s_split, n * 2)
                    else:
                        pe.wait_ge(s_cleared, h + 1)
                    split_product(o_ps, gla_q(q_hi, p, 0), gla_q(q_lo, p, 0), s_hi[:, 0, :], s_lo[:, 0, :], False, False)
                    pe.wait_ge(s_split, n * 2 + 1)
                    split_product(o_ps, gla_q(q_hi, p, 1), gla_q(q_lo, p, 1), s_hi[:, 1, :], s_lo[:, 1, :],
                                  False, True).then_inc(o_ready, 1)

            gla_qkv(Unit(U_QKV0), 0, False)
            with pe.Fori(0, HEADS - 1) as h:
                gla_steps(Unit(U_HEAD, 6, h), h)
                gla_qkv(Unit(U_HEAD + 2, 6, h), h + 1, True)
            gla_steps(Unit(U_G3), HEADS - 1)

            project(Unit(U_YA), h_hi, h_lo)
            gla_final(HEADS - 1)
            project(Unit(U_YA + 1), og_hi, og_lo, wait_k=og_split)
            with pe.Fori(1, KD) as c:
                u = Unit(U_YA, 2, c)
                project(u, h_hi, h_lo)
                project(u + 1, og_hi, og_lo)

            with pe.Fori(0, LGROUPS) as g:
                for r in range(6):
                    project(lru_unit(g, r), h_hi, h_lo, n=LT)
                wa, wx = lru_unit(g, 6), lru_unit(g, 7)
                pe.wait_ge(xc_split, g * 3 + 3)
                for o in range(3):
                    tiles = range(max(0, o - 1), min(2, o + 1) + 1)
                    for u, ps, ready, free in ((wa, pp[2], ra_ready, ra_free), (wx, pp[3], rx_ready, rx_free)):
                        if o:
                            pe.wait_ge(free, g * 3 + o)
                        else:
                            pe.wait_ge(w_split, u.done())
                        for half in range(2):
                            tok = slice(half * HALF, (half + 1) * HALF)
                            for k in tiles:
                                c0 = k * 3 * LT + o * LT
                                last = split_product(
                                    ps[0:LT, tok], w_hi[0:LT, u.slot(), c0:c0 + LT], w_lo[0:LT, u.slot(), c0:c0 + LT],
                                    xc_hi[:, k, tok], xc_lo[:, k, tok], k == tiles[0], k == tiles[-1])
                        if u is wa and o == 2:
                            last.then_inc(unit_done, 1)
                        else:
                            last.then_inc(ready, 1)
                pe.wait_ge(rx_ready, g * 3 + 3)
                pe.sem_inc(unit_done, 1)

            with pe.Fori(0, KD // 2) as c:
                for r in range(2):
                    project(late_unit(U_GB + r, 2, c), h_hi, h_lo)
            pe.wait_ge(rx_free, LTILES)
            with pe.Fori(0, KD // 2) as c:
                for n in range(2):
                    for r in range(2):
                        u = late_unit(U_YB + 2 * n + r, 4, c)
                        pe.wait_ge(w_split, u.done())
                        for k in range(6):
                            pe.wait_ge(hl_split, 6 * r + k + 1)
                            for half in range(2):
                                tok = slice(half * HALF, (half + 1) * HALF)
                                last = split_product(pp[2 + n][:, tok], *weights(u, k, P, LT), hl_hi[:, 6 * r + k, tok],
                                                     hl_lo[:, 6 * r + k, tok], r + k == 0, r == 1 and k == 5)
                        last.then_inc(unit_done, 1)

            def contract(a_hi, a_lo, nk, u0, nth, free):
                for half in range(2):
                    def step(kk, r, first=False, final=False):
                        u = late_unit(u0 + half * nk + 2 * kk + r) if isinstance(kk, int) else \
                            late_unit(u0 + half * nk + r, 2, kk)
                        pe.wait_ge(w_split, u.done())
                        pe.wait_ge(a_split, kk * 2 + (nth + half * nk + r + 1))
                        for t in range(4):
                            if first and half:
                                pe.wait_ge(acc_stored, nth // (2 * KD) * KD + t + 1)
                            elif first:
                                for wait in free[t]:
                                    pe.wait_ge(*wait)
                            tok = slice(t * P, (t + 1) * P)
                            for c in range(2):
                                col = slice(c * HALF, (c + 1) * HALF)
                                last = split_product(
                                    pp[t][:, col], a_hi[:, u.slot(), tok], a_lo[:, u.slot(), tok],
                                    w_hi[:, u.slot(), col], w_lo[:, u.slot(), col], first, final)
                        last.then_inc(unit_done, 1)
                    step(0, 0, first=True)
                    step(0, 1)
                    with pe.Fori(1, nk // 2 - 1) as kk:
                        step(kk, 0)
                        step(kk, 1)
                    step(nk // 2 - 1, 0)
                    step(nk // 2 - 1, 1, final=True)

            contract(ao_hi, ao_lo, KD, U_OUT, 0,
                     [[(ps_free[0], gb_uses(0))], [(ps_free[1], gb_uses(1))], [(yb_free[0], 4)], [(yb_free[1], 4)]])
            transpose_tiles(xn2, KD, (acc_stored, KD))
            pe.wait_ge(xT_split, 2 * KD)

            with pe.Fori(0, FT) as j:
                for n in range(2):
                    project(late_unit(U_UP + n, 2, j, apart=LGROUPS + 2 * KD), g_hi, g_lo)
            up_uses = [gb_uses(n) + FT for n in range(2)]
            contract(ad_hi, ad_lo, FT, U_DN, 2 * KD,
                     [[(ps_free[0], up_uses[0])], [(ps_free[1], up_uses[1])], [], []])


_INS = ["x", "attn_norm", "w_in", "gla_wf2", "gla_bf2", "gla_onorm", "gla_wo", "lru_conv_w", "lru_conv_b",
        "lru_wa", "lru_ba", "lru_wx", "lru_bx", "lru_a_param", "lru_wo", "w_out", "ffn_norm", "ffn_wup",
        "ffn_conv_w", "ffn_conv_b", "ffn_wdown", "final_norm"]


def kernel(**inputs):
    import numpy as _np
    import concourse.bacc as _bacc
    from concourse import mybir as _mybir
    from concourse.bass_utils import run_bass_kernel_spmd as _run

    nc = _bacc.Bacc("TRN2", target_bir_lowering=False, num_devices=1)
    arrays, args = {}, []
    for name in _INS:
        a = _np.ascontiguousarray(inputs[name])
        arrays[f"in_{name}_dram"] = a
        args.append(nc.dram_tensor(f"in_{name}_dram", a.shape, _mybir.dt.from_np(a.dtype), kind="ExternalInput").ap())
    out = nc.dram_tensor("out_dram", (1, S, D), _mybir.dt.float32, kind="ExternalOutput").ap()
    build(nc, *args, out)
    r = _run(nc, [arrays], core_ids=[0])
    return r.results[0]["out_dram"]
```

```python
from contextlib import ExitStack

import concourse.bass as bass
from concourse import mybir

F32 = mybir.dt.float32
F32R = mybir.dt.float32r
ALU = mybir.AluOpType
ACT = mybir.ActivationFunctionType

P = 128
D = 1024
S = 1024
KD = D // P
HALF = 512
EPS = 1e-6

HEADS, DK, DV, CHUNK = 4, 128, 256, 64
RANK = 16
PAIRS = S // P
GATE_NORM = 16.0
LW = 1344
BW = LW // 8
LT = 112
LTILES = LW // LT
LGROUPS = LTILES // 3
FF = 3 * D
FT = FF // P

C_Q = 0
C_K = C_Q + HEADS * DK
C_V = C_K + HEADS * DK
C_G = C_V + HEADS * DV
C_F = C_G + HEADS * DV
C_LX = C_F + RANK
C_LG = C_LX + LW
C_GA = C_LG + LW
C_GB = C_GA + D

U_F = 0
U_QKV0 = 1
U_HEAD = U_QKV0 + 4
U_G3 = U_HEAD + 6 * (HEADS - 1)
U_YA = U_G3 + 2
U_LRU = U_YA + 2 * KD
U_GB = U_LRU + 8 * LGROUPS
U_YB = U_GB + KD
U_OUT = U_YB + 2 * KD
U_UP = U_OUT + 2 * KD
U_DN = U_UP + 2 * FT
U_END = U_DN + 2 * FT

A_NORM, A_BF2, A_ONORM, A_FNORM, A_FB, A_W2 = 0, 8, 12, 14, 22, 70
N_A = A_W2 + 2 * FT
N_B = 4 * FT
L_W, L_B, L_BA, L_BX, L_AP = 0, 4 * LTILES, 5 * LTILES, 6 * LTILES, 7 * LTILES
N_L = 8 * LTILES


class Unit:

    def __init__(self, const, per=0, i=None, extra=(0, 0), apart=(0, 0)):
        self.const, self.per, self.i, self.extra, self.apart = const, per, i, extra, apart

    def __add__(self, n):
        return Unit(self.const + n, self.per, self.i, self.extra, self.apart)

    def value(self, const, per):
        return const if self.i is None else self.i * per + const

    def slot(self):
        return self.const % 2

    def done(self, n=1):
        return self.value(self.const + n, self.per)

    def loaded(self):
        return self.value(16 * (self.const // 2 + 1 + 3 * self.extra[0]), 8 * self.per + 48 * self.extra[1])

    def ps(self, n=0):
        return self.value(self.const // 2 + n - self.apart[0], self.per // 2 - self.apart[1])


def lru_unit(g, r):
    return Unit(U_LRU + r, 8, g, extra=(int(r >= 6), 1), apart=(int(r >= 8), 1))


def ffn_unit(j):
    apart = LGROUPS + 2 * KD
    return late_unit(U_UP + 2 * j, apart=apart) if isinstance(j, int) else late_unit(U_UP, 2, j, apart=apart)


def gb_uses(slot):
    return sum(1 for u in range(U_YB) if u % 2 == slot) - LGROUPS


def late_unit(const, per=0, i=None, apart=LGROUPS):
    return Unit(const, per, i, extra=(LGROUPS, 0), apart=(apart, 0))


class Order:

    def __init__(self, eng, sem):
        self.eng, self.sem, self.base, self.n = eng, sem, 0, 0

    def after(self, ins):
        ins.then_inc(self.sem, 1)
        self.n += 1
        self.eng.wait_ge(self.sem, self.base + self.n)

    def enter(self, i, per):
        self.saved = (self.base, self.n, per)
        self.base, self.n = i * per + (self.base + self.n), 0

    def leave(self, times):
        base, n, per = self.saved
        assert self.n == per, (self.n, per)
        self.base, self.n = base + n + per * times, 0


def build(nc, x, attn_norm, w_in, gla_wf2, gla_bf2, gla_onorm, gla_wo, lru_conv_w, lru_conv_b,
          lru_wa, lru_ba, lru_wx, lru_bx, lru_a_param, lru_wo, w_out, ffn_norm, ffn_wup,
          ffn_conv_w, ffn_conv_b, ffn_wdown, final_norm, out):
    ds = bass.ds
    ctx = ExitStack()
    with ctx:
        def sb(name, shape, dt=F32, scope=ctx):
            return scope.enter_context(nc.sbuf_tensor(name, shape, dt))

        def sem(name):
            return ctx.enter_context(nc.semaphore(name))

        vec_a = sb("vec_a", [P, N_A])
        vec_b = sb("vec_b", [P, N_B])
        vec_l = sb("vec_l", [LT, N_L])
        ident = sb("ident", [P, P])
        causal = sb("causal", [P, P])
        ones = sb("ones", [P, CHUNK])
        onorm_half = sb("onorm_half", [P, 2])
        sp2 = sb("sp2", [LT, LTILES])
        minus_sp4 = sb("minus_sp4", [LT, LTILES])
        half_b = sb("half_b", [LT, 2 * LTILES])
        soft = sb("soft", [LT, 4, LTILES])
        sumsq = sb("sumsq", [P, 8])
        ms = sb("ms", [P, 8])
        rs = sb("rs", [P, 8])
        newton = sb("newton", [P, 8])
        wf_raw = sb("wf_raw", [RANK, HEADS * DK])
        w_raw = sb("w_raw", [P, 2, 1024])
        w_hi = sb("w_hi", [P, 2, 1024], F32R)
        w_lo = sb("w_lo", [P, 2, 1024], F32R)

        h_scope = ExitStack()
        h_hi = sb("h_hi", [P, KD, S], F32R, h_scope)
        h_lo = sb("h_lo", [P, KD, S], F32R, h_scope)

        xs = ExitStack()
        x_in = sb("x_in", [P, KD, S], scope=xs)
        xn1 = sb("xn1", [P, 2, S], scope=xs)
        xr1 = sb("xr1", [P, 2, S], scope=xs)
        junk1 = sb("junk1", [P, S], scope=xs)
        rows_a = sb("rows_a", [N_A, P], scope=xs)
        rows_b = sb("rows_b", [N_B, P], scope=xs)
        rows_l = sb("rows_l", [N_L, LT], scope=xs)
        xs.close()

        og_scope = ExitStack()
        og_raw = sb("og_raw", [P, KD, S], scope=og_scope)
        gla = ExitStack()
        f_hi = sb("f_hi", [RANK, S], F32R, gla)
        f_lo = sb("f_lo", [RANK, S], F32R, gla)
        wf_hi = sb("wf_hi", [RANK, DK], F32R, gla)
        wf_lo = sb("wf_lo", [RANK, DK], F32R, gla)
        k_hi = sb("k_hi", [P, S], F32R, gla)
        k_lo = sb("k_lo", [P, S], F32R, gla)
        cum = sb("cum", [P, S], scope=gla)
        g1 = sb("g1", [P, S], scope=gla)
        g2 = sb("g2", [P, S], scope=gla)
        ks = sb("ks", [P, S], scope=gla)
        vo = sb("vo", [P, PAIRS, DV], scope=gla)
        sg = sb("sg", [P, 2, S], scope=gla)
        decay = sb("decay", [P, S // CHUNK], scope=gla)
        kt_hi = sb("kt_hi", [P, 2, P], F32R, gla)
        kt_lo = sb("kt_lo", [P, 2, P], F32R, gla)
        v_hi = sb("v_hi", [P, 2, DV], F32R, gla)
        v_lo = sb("v_lo", [P, 2, DV], F32R, gla)
        at_raw = sb("at_raw", [P, P], scope=gla)
        at_hi = sb("at_hi", [P, P], F32R, gla)
        at_lo = sb("at_lo", [P, P], F32R, gla)
        s_raw = sb("s_raw", [P, DV], scope=gla)
        s_hi = sb("s_hi", [P, 2, DV], F32R, gla)
        s_lo = sb("s_lo", [P, 2, DV], F32R, gla)
        squares = sb("squares", [P, DV], scope=gla)
        q_hi = sb("q_hi", [P, PAIRS * 256 + P], F32R, gla)
        q_lo = sb("q_lo", [P, PAIRS * 256 + P], F32R, gla)
        gla.close()
        og_scope.close()
        ya = ExitStack()
        og_lo = sb("og_lo", [P, KD, S], F32R, ya)
        og_hi = sb("og_hi", [P, KD, S], F32R, ya)
        m_a = sb("m_a", [P, KD, S], scope=ya)
        t_a = sb("t_a", [P, S], scope=ya)
        ya.close()
        lru = ExitStack()
        hl = sb("hl", [LT, LTILES, S], scope=lru)
        xc_hi = sb("xc_hi", [LT, 3, S], F32R, lru)
        xc_lo = sb("xc_lo", [LT, 3, S], F32R, lru)
        conv = sb("conv", [LT, S], scope=lru)
        lw = sb("lw", [LT, 3, S], scope=lru)
        la = sb("la", [LT, 3, S], scope=lru)
        lc = sb("lc", [LT, 3, S], scope=lru)
        lru.close()
        mg = ExitStack()
        hl_lo = sb("hl_lo", [LT, LTILES, S], F32R, mg)
        t_b = sb("t_b", [P, KD, S], scope=mg)
        m = sb("m", [P, KD, S], scope=mg)
        mg.close()
        oscope = ExitStack()
        x2 = sb("x2", [P, KD, S], scope=oscope)
        xn2 = sb("xn2", [P, 2, S], scope=oscope)
        xr2 = sb("xr2", [P, 2, S], scope=oscope)
        junk2 = sb("junk2", [P, S], scope=oscope)
        oscope.close()
        fscope = ExitStack()
        hid = sb("hid", [P, FT, S], scope=fscope)
        ug = sb("ug", [P, S], scope=fscope)
        uv = sb("uv", [P, S], scope=fscope)
        ad_hi = sb("ad_hi", [P, 2, HALF], F32R, fscope)
        ad_lo = sb("ad_lo", [P, 2, HALF], F32R, fscope)
        fscope.close()

        h_scope.close()
        h2 = ExitStack()
        hl_hi = sb("hl_hi", [LT, LTILES, S], F32R, h2)
        yb = sb("yb", [P, S], scope=h2)
        ao_hi = sb("ao_hi", [P, 2, HALF], F32R, h2)
        ao_lo = sb("ao_lo", [P, 2, HALF], F32R, h2)
        h2.close()
        h3 = ExitStack()
        g_hi = sb("g_hi", [P, KD, S], F32R, h3)
        g_lo = sb("g_lo", [P, KD, S], F32R, h3)
        h3.close()
        h4 = ExitStack()
        y = sb("y", [P, KD, S], scope=h4)
        final_gain = sb("final_gain", [P, D], scope=h4)
        junk = sb("junk", [P, S], scope=h4)
        h4.close()

        pp = [ctx.enter_context(nc.psum_tensor(f"pp{i}", [P, 1024], F32)) for i in range(4)]
        at_ps, o_ps = pp[2][:, 0:P], pp[2][:, HALF:HALF + DV]
        tr_ps, ds_ps = pp[3][:, 0:P + DV], pp[3][:, HALF:2 * HALF]

        m_dram = nc.dram_tensor("m_scratch", [P, KD, S], F32, kind="Internal").ap()
        x2_dram = nc.dram_tensor("x2_scratch", [P, KD, S], F32, kind="Internal").ap()

        w_rounded = sem("w_rounded")
        w_split = sem("w_split")
        unit_done = sem("unit_done")
        zeroed = sem("zeroed")
        act_order = sem("act_order")
        dve_order = sem("dve_order")
        setup = sem("setup")
        rows_loaded = sem("rows_loaded")
        vecs_T = sem("vecs_T")
        vecs = sem("vecs")
        soft_abs = sem("soft_abs")
        soft_e = sem("soft_e")
        squared = sem("squared")
        ms_ready = sem("ms_ready")
        rs0_ready = sem("rs0_ready")
        rs_ready = sem("rs_ready")
        xn_ready = sem("xn_ready")
        xT_ready = sem("xT_ready")
        xr_ready = sem("xr_ready")
        xr_rounded = sem("xr_rounded")
        xT_split = sem("xT_split")
        wf_ready = sem("wf_ready")
        z_ready = sem("z_ready")
        z_abs = sem("z_abs")
        z_free = sem("z_free")
        sp_ready = sem("sp_ready")
        cum_ready = sem("cum_ready")
        bdiff_ready = sem("bdiff_ready")
        gates_ready = sem("gates_ready")
        qk_rounded = sem("qk_rounded")
        qk_split = sem("qk_split")
        tr_ready = sem("tr_ready")
        kv_rounded = sem("kv_rounded")
        kv_split = sem("kv_split")
        at_ready = sem("at_ready")
        at_masked = sem("at_masked")
        at_rounded = sem("at_rounded")
        at_split = sem("at_split")
        ds_ready = sem("ds_ready")
        s_cleared = sem("s_cleared")
        s_updated = sem("s_updated")
        s_rounded = sem("s_rounded")
        s_split = sem("s_split")
        o_ready = sem("o_ready")
        o_stored = sem("o_stored")
        g_tanh = sem("g_tanh")
        on_ready = sem("on_ready")
        oT_ready = sem("oT_ready")
        og_ready = sem("og_ready")
        og_rounded = sem("og_rounded")
        og_split = sem("og_split")
        m_stored = sem("m_stored")
        m_loaded = sem("m_loaded")
        m_ready = sem("m_ready")
        xc_split = sem("xc_split")
        ra_ready = sem("ra_ready")
        rx_ready = sem("rx_ready")
        ra_free = sem("ra_free")
        rx_free = sem("rx_free")
        gated = sem("gated")
        lru_act = sem("lru_act")
        lru_out = sem("lru_out")
        hl_rounded = sem("hl_rounded")
        hl_split = sem("hl_split")
        a_rounded = sem("a_rounded")
        a_split = sem("a_split")
        tile_done = sem("tile_done")
        acc_stored = sem("acc_stored")
        xres_loaded = [sem("xres_loaded0"), sem("xres_loaded1")]
        x2_saved = sem("x2_saved")
        x2_loaded = [sem("x2_loaded0"), sem("x2_loaded1")]
        u_first = sem("u_first")
        u_gelu = sem("u_gelu")
        hid_ready = sem("hid_ready")
        y_ready = sem("y_ready")
        out_saved = sem("out_saved")
        slots_freed, gate_slots_freed = sem("slots_freed"), sem("gate_slots_freed")
        w_loaded = [sem("w_loaded0"), sem("w_loaded1")]
        ps_free = [sem("ps_free0"), sem("ps_free1")]
        yb_free = [sem("yb_free0"), sem("yb_free1")]
        x_loaded = [sem(f"x_loaded{i}") for i in range(KD)]

        block = ctx.enter_context(nc.Block())

        def token_tile(i):
            return i // 4 * 4 + (2, 3, 0, 1)[i % 4]

        def gla_q(t, p, c):
            return t[:, p * 256 + c * P:p * 256 + (c + 1) * P]

        def gla_q_tokens(t, p):
            return t[:, p * 256:p * 256 + 384].rearrange("a (c x) -> a c x", x=192)[:, :, 0:CHUNK]

        def q_chunks(t, c):
            return t[:, 0:PAIRS * 256].rearrange("a (p x) -> a p x", x=256)[
                :, :, c * 192:c * 192 + CHUNK]

        def chunks(t, c):
            return t[:, :].rearrange("a (p x) -> a p x", x=P)[:, :, c * CHUNK:(c + 1) * CHUNK]

        def f32(ap):
            return ap.bitcast(F32)

        def cols(src, c0, n):
            return src[0].rearrange("(k p) e -> p k e", p=P)[:, :, ds(c0, n)]

        @block.sync
        def _(sp):
            for t in range(4):
                sp.dma_start(x_in[:, t, :], x[0, t * P:(t + 1) * P, :]).then_inc(x_loaded[t], 16)
            sp.dma_start(rows_a[A_NORM:A_BF2, :], attn_norm[0].rearrange("(k p) -> k p", p=P)).then_inc(rows_loaded, 16)
            sp.dma_start(rows_a[A_BF2:A_ONORM, :], gla_bf2[0].rearrange("(k p) -> k p", p=P)).then_inc(rows_loaded, 16)
            sp.dma_start(rows_a[A_ONORM:A_FNORM, :], gla_onorm[0].rearrange("(k p) -> k p", p=P)).then_inc(rows_loaded, 16)
            sp.dma_start(rows_a[A_FNORM:A_FB, :], ffn_norm[0].rearrange("(k p) -> k p", p=P)).then_inc(rows_loaded, 16)
            sp.dma_start(rows_a[A_FB:A_W2, :], ffn_conv_b[0].rearrange("(k p) -> k p", p=P)).then_inc(rows_loaded, 16)
            sp.dma_start(rows_a[A_W2:N_A, :], ffn_conv_w[0, 2].rearrange("(k p) -> k p", p=P)).then_inc(rows_loaded, 16)
            sp.dma_start(rows_b[:, :], ffn_conv_w[0, 0:2].rearrange("t (k p) -> (t k) p", p=P)).then_inc(rows_loaded, 16)
            sp.dma_start(rows_l[L_W:L_B, :], lru_conv_w[0].rearrange("t (k p) -> (t k) p", p=LT)).then_inc(rows_loaded, 16)
            for at, v in ((L_B, lru_conv_b), (L_BA, lru_ba), (L_BX, lru_bx), (L_AP, lru_a_param)):
                sp.dma_start(rows_l[at:at + LTILES, :], v[0].rearrange("(k p) -> k p", p=LT)).then_inc(rows_loaded, 16)
            sp.dma_start(wf_raw[:, :], gla_wf2[0]).then_inc(rows_loaded, 16)
            for t in range(4, KD):
                sp.dma_start(x_in[:, t, :], x[0, t * P:(t + 1) * P, :]).then_inc(x_loaded[t], 16)

            def load(u, src, rows=P, shape=None):
                if u.const >= 2:
                    sp.wait_ge(w_split, u.done(-1))
                    sp.sem_inc(slots_freed, 1)
                else:
                    sp.wait_ge(setup, 4)
                dst = w_raw[0:rows, u.slot(), :]
                if shape:
                    dst = dst[:, 0:shape[0] * shape[1]].rearrange("p (a b) -> p a b", b=shape[1])
                sp.dma_start(dst, src).then_inc(w_loaded[u.slot()], 16)

            def load_cols(u, w, c0, n=P):
                load(u, cols(w, c0, n), shape=(KD, n))

            load_cols(Unit(U_F), w_in, C_F, RANK)

            def load_qkv(u, h):
                load_cols(u, w_in, h * DK + C_Q)
                load_cols(u + 1, w_in, h * DK + C_K)
                load_cols(u + 2, w_in, h * DV + C_V)
                load_cols(u + 3, w_in, h * DV + (C_V + P))

            def load_g(u, h):
                load_cols(u, w_in, h * DV + C_G)
                load_cols(u + 1, w_in, h * DV + (C_G + P))

            load_qkv(Unit(U_QKV0), 0)
            with sp.Fori(0, HEADS - 1) as h:
                u = Unit(U_HEAD, 6, h)
                load_g(u, h)
                load_qkv(u + 2, h + 1)
            load_g(Unit(U_G3), HEADS - 1)
            with sp.Fori(0, KD) as c:
                u = Unit(U_YA, 2, c)
                load_cols(u, w_in, c * P + C_GA)
                load_cols(u + 1, gla_wo, c * P)

            with sp.Fori(0, LGROUPS) as g:
                for r in range(6):
                    c0 = (C_LX if r < 3 else C_LG) + (r % 3) * LT
                    load_cols(lru_unit(g, r), w_in, g * (3 * LT) + c0, LT)
                for r, wg in ((6, lru_wa), (7, lru_wx)):
                    u = lru_unit(g, r)
                    sp.wait_ge(zeroed, g * 2 + (r - 5))
                    sp.sem_inc(slots_freed, 1)
                    w = w_raw[:, u.slot(), 0:3 * 3 * LT].rearrange("p (k c) -> p k c", c=3 * LT)
                    low = wg[0, ds(g * 2, 1), :, :].rearrange("b i o -> (b i) o")
                    high = wg[0, ds(g * 2 + 1, 1), :, :].rearrange("b i o -> (b i) o")
                    cut = BW - LT
                    for dst, src in ((w[0:LT, 0, 0:BW], low[0:LT, :]), (w[0:cut, 1, 0:BW], low[LT:BW, :]),
                                     (w[cut:LT, 1, BW:2 * BW], high[0:cut, :]),
                                     (w[0:LT, 2, BW:2 * BW], high[cut:BW, :])):
                        sp.dma_start(dst, src).then_inc(w_loaded[u.slot()], 16)

            with sp.Fori(0, KD // 2) as c:
                for r in range(2):
                    load_cols(Unit(U_GB + r, 2, c), w_in, c * (2 * P) + (C_GB + r * P))
            with sp.Fori(0, KD) as c:
                for r in range(2):
                    half = lru_wo[0, r * (LW // 2):(r + 1) * (LW // 2), :]
                    load(Unit(U_YB + r, 2, c), half.rearrange("(k p) e -> p k e", p=LT)[:, :, ds(c * P, P)],
                         rows=LT, shape=(LTILES // 2, P))

            def load_rows(u0, w, nk):
                with sp.Fori(0, nk // 2) as kk:
                    for r in range(2):
                        load(Unit(u0 + r, 2, kk), w[0, ds(kk * (2 * P) + r * P, P), :])

            for half in range(2):
                load_rows(U_OUT + half * KD, w_out, KD)
            with sp.Fori(0, FT) as j:
                for r in range(2):
                    load_cols(Unit(U_UP + r, 2, j), ffn_wup, j * P + r * FF)
            for half in range(2):
                load_rows(U_DN + half * FT, ffn_wdown, FT)

        @block.gpsimd
        def _(pool):
            nc.gpsimd.memset(ident[:, :], 0.0).then_inc(setup, 1)
            nc.gpsimd.memset(causal[:, :], 1.0).then_inc(setup, 1)
            nc.gpsimd.memset(ones[:, :], 1.0).then_inc(setup, 1)
            nc.gpsimd.memset(w_raw[:, :, :], 0.0).then_inc(setup, 1)
            pool.wait_ge(setup, 4)
            nc.gpsimd.affine_select(out=ident[:, :], in_=ident[:, :], compare_op=ALU.not_equal, fill=1.0,
                                    base=0, pattern=[[-1, P]], channel_multiplier=1).then_inc(setup, 1)
            nc.gpsimd.affine_select(out=causal[:, :], in_=causal[:, :], compare_op=ALU.is_ge, fill=0.0,
                                    base=0, pattern=[[1, P]], channel_multiplier=-1).then_inc(setup, 1)
            pool.wait_ge(setup, 6)
            nc.gpsimd.memset(causal[0:CHUNK, CHUNK:P], 0.0).then_inc(setup, 1)
            for t in (at_raw[:, :], f32(q_hi[:, :]), f32(q_lo[:, :]), f32(kt_hi[:, :, :]), f32(kt_lo[:, :, :])):
                nc.gpsimd.memset(t, 0.0).then_inc(setup, 1)

            with pool.Fori(0, KD) as c:
                wo = Unit(U_YA + 1, 2, c)
                pool.wait_ge(ps_free[wo.slot()], wo.ps(1))
                pool.dma_start(m_dram[:, ds(c, 1), :], m_a[:, ds(c, 1), :]).then_inc(m_stored, 16)
            with pool.Fori(0, LGROUPS) as g:
                for r in (6, 7):
                    u = lru_unit(g, r)
                    pool.wait_ge(w_split, u.done(-1))
                    pool.sem_inc(gate_slots_freed, 1)
                    nc.gpsimd.memset(w_raw[:, u.slot(), :], 0.0).then_inc(zeroed, 1)
            pool.wait_ge(m_stored, 16 * KD)
            pool.wait_ge(lru_out, LTILES)
            pool.dma_start(m[:, :, :], m_dram[:, :, :]).then_inc(m_loaded, 16)
            pool.wait_ge(m_ready, KD)
            for i in range(KD):
                t = token_tile(i)
                if i:
                    pool.wait_ge(unit_done, U_OUT + i)
                pool.dma_start(x2[:, t, :], x[0, t * P:(t + 1) * P, :]).then_inc(xres_loaded[i // 4], 16)
            for i in range(KD):
                t = token_tile(i)
                pool.wait_ge(acc_stored, i + 1)
                pool.dma_start(x2_dram[:, t, :], x2[:, t, :]).then_inc(x2_saved, 16)
            pool.wait_ge(x2_saved, 16 * KD)
            pool.wait_ge(unit_done, U_DN)
            pool.dma_start(final_gain[:, :], final_norm.partition_broadcast(P)).then_inc(x2_loaded[0], 16)
            for i in range(KD):
                t = token_tile(i)
                pool.wait_ge(unit_done, U_DN + 3 * i)
                pool.dma_start(y[:, t, :], x2_dram[:, t, :]).then_inc(x2_loaded[i // 4], 16)
            for i in range(KD):
                t = token_tile(i)
                pool.wait_ge(y_ready, i + 1)
                pool.dma_start(out[0, t * P:(t + 1) * P, :], y[:, t, :]).then_inc(out_saved, 16)
            pool.wait_ge(out_saved, 16 * KD)

        @block.scalar
        def _(act):
            order = Order(act, act_order)
            fn = nc.scalar.activation

            def round_unit(u):
                act.wait_ge(w_loaded[u.slot()], u.loaded())
                if u.const >= 2:
                    act.wait_ge(unit_done, u.done(-1))
                fn(w_hi[:, u.slot(), :], w_raw[:, u.slot(), :], ACT.Copy).then_inc(w_rounded, 1)

            def rsqrt_seed(n0, n1, nth):
                act.wait_ge(ms_ready, nth)
                order.after(fn(rs[:, n0:n1], ms[:, n0:n1], ACT.Ln))
                fn(rs[:, n0:n1], rs[:, n0:n1], ACT.Exp, scale=-0.5).then_inc(rs0_ready, 1)

            def round_transposed(dst, xr, t, nth):
                act.wait_ge(xr_ready, nth)
                fn(dst[:, :, t * P:(t + 1) * P], xr[:, t % 2, :].rearrange("p (k c) -> p k c", c=P),
                   ACT.Copy).then_inc(xr_rounded, 1)

            def norm_transposed(square, src, xn, xr, dst, base, rs_base, seed_nth, units):
                def scale(t):
                    act.wait_ge(rs_ready, rs_base + 1 + t // 4)
                    if t >= 2:
                        act.wait_ge(xT_ready, base + t - 1)
                    fn(xn[:, t % 2, :], src[:, t, :], ACT.Identity, scale=rs[:, t:t + 1]).then_inc(xn_ready, 1)

                scale(0)
                scale(1)
                for t in range(KD):
                    if t == 0:
                        square(4)
                    if t + 2 < KD:
                        scale(t + 2)
                    round_transposed(dst, xr, t, base + t + 1)
                    if t == 0:
                        square(5)
                        square(6)
                    if t == 1:
                        square(7)
                        rsqrt_seed(4, 8, seed_nth)
                    if t in (2, 3) and t - 2 >= 2 - len(units):
                        round_unit(units[t - 4])

            def square1(t):
                act.wait_ge(x_loaded[t], 16)
                if t:
                    act.wait_ge(squared, t)
                fn(junk1[:, :], x_in[:, t, :], ACT.Square, accum_out=sumsq[:, t:t + 1]).then_inc(squared, 1)

            for t in range(4):
                square1(t)
            rsqrt_seed(0, 4, 1)
            act.wait_ge(vecs, 3)
            fn(soft[:, 0, :], vec_l[:, L_AP:N_L], ACT.Abs).then_inc(soft_abs, 1)
            act.wait_ge(soft_abs, 1)
            fn(soft[:, 0, :], soft[:, 0, :], ACT.Exp, scale=-1.0).then_inc(soft_e, 1)
            norm_transposed(square1, x_in, xn1, xr1, h_hi, 0, 0, 2, [Unit(U_F), Unit(U_QKV0)])

            def gla_gate(u, h, d):
                act.wait_ge(unit_done, (u + d).done())
                fn(sg[:, d, :], pp[(u + d).slot()][:, :], ACT.Tanh, scale=0.5).then_inc(g_tanh, 1)

            def gla_qkv(u, h, final):
                round_unit(u + 1)
                act.wait_ge(z_ready, h + 1)
                fn(g1[:, :], pp[2][:, :], ACT.Abs, bias=vec_a[:, ds(h + A_BF2, 1)]).then_inc(z_abs, 1)
                act.wait_ge(z_abs, h + 1)
                order.after(fn(g1[:, :], g1[:, :], ACT.Exp, scale=-1.0))
                fn(g1[:, :], g1[:, :], ACT.Ln, bias=1.0).then_inc(sp_ready, 1)
                if final:
                    rsqrt_seed(0, PAIRS, h + 2)
                act.wait_ge(cum_ready, h + 1)
                fn(g1[:, :], cum[:, :], ACT.Exp, scale=1.0 / GATE_NORM).then_inc(gates_ready, 1)
                fn(g2[:, :], cum[:, :], ACT.Exp, scale=-1.0 / GATE_NORM).then_inc(gates_ready, 1)
                fn(decay[:, :], cum[:, CHUNK - 1:S:CHUNK], ACT.Exp, scale=1.0 / GATE_NORM)
                act.wait_ge(bdiff_ready, h + 1)
                fn(ks[:, :], ks[:, :], ACT.Exp, scale=1.0 / GATE_NORM).then_inc(gates_ready, 1)
                act.wait_ge(ps_free[u.slot()], u.ps(1))
                fn(q_chunks(q_hi, 0), chunks(g1, 0), ACT.Copy)
                fn(q_chunks(q_hi, 1), chunks(g1, 1), ACT.Copy).then_inc(qk_rounded, 1)
                round_unit(u + 2)
                act.wait_ge(ps_free[(u + 1).slot()], (u + 1).ps(1))
                fn(k_hi[:, :], g2[:, :], ACT.Copy).then_inc(qk_rounded, 1)
                round_unit(u + 3)
                for d in range(2):
                    v = u + (2 + d)
                    act.wait_ge(unit_done, v.done())
                    if d == 0 and final:
                        act.wait_ge(oT_ready, h * 2)
                    fn(vo[:, :, d * P:(d + 1) * P], pp[v.slot()][:, :].rearrange("p (n c) -> p n c", c=P),
                       ACT.Copy).then_inc(ps_free[v.slot()], 1)
                    if d == 0:
                        round_unit(u + 4)

            def gla_steps(u, h):
                def round_kv(p):
                    act.wait_ge(tr_ready, h * PAIRS + (p + 1))
                    fn(kt_hi[0:CHUNK, 0, :], tr_ps[0:CHUNK, 0:P], ACT.Copy)
                    fn(kt_hi[CHUNK:P, 1, :], tr_ps[CHUNK:P, 0:P], ACT.Copy)
                    fn(v_hi[:, p % 2, :], tr_ps[:, P:], ACT.Copy).then_inc(kv_rounded, 1)

                round_kv(0)
                for p in range(PAIRS):
                    n = h * PAIRS + p
                    act.wait_ge(at_masked, n + 1)
                    fn(at_hi[:, :], at_raw[:, :], ACT.Copy).then_inc(at_rounded, 1)
                    act.wait_ge(s_updated, n * 2 + 1)
                    fn(s_hi[:, 1, :], s_raw[:, :], ACT.Copy).then_inc(s_rounded, 1)
                    if p + 1 < PAIRS:
                        round_kv(p + 1)
                    if p % 4 == 0:
                        round_unit(u + (1 + p // 4))
                    if p == 5:
                        gla_gate(u, h, 0)
                    act.wait_ge(o_ready, n + 1)
                    order.after(fn(vo[:, p, :], o_ps, ACT.Copy))
                    fn(squares[:, :], vo[:, p, :], ACT.Square, accum_out=sumsq[:, p:p + 1]).then_inc(o_stored, 1)
                    act.wait_ge(s_updated, n * 2 + 2)
                    fn(s_hi[:, 0, :], s_raw[:, :], ACT.Copy).then_inc(s_rounded, 1)
                gla_gate(u, h, 1)

            gla_qkv(Unit(U_QKV0), 0, False)
            with act.Fori(0, HEADS - 1) as h:
                order.enter(h, PAIRS + 2)
                gla_steps(Unit(U_HEAD, 6, h), h)
                gla_qkv(Unit(U_HEAD + 2, 6, h), h + 1, True)
            order.leave(HEADS - 1)
            gla_steps(Unit(U_G3), HEADS - 1)
            rsqrt_seed(0, PAIRS, 2 + HEADS)

            round_unit(Unit(U_YA + 1))
            for k in range(2 * HEADS):
                if k == 2 * (HEADS - 1):
                    act.wait_ge(og_ready, 2 * HEADS)
                fn(og_hi[:, k, :], og_raw[:, k, :], ACT.Copy).then_inc(og_rounded, 1)
            with act.Fori(0, KD) as c:
                u = Unit(U_YA, 2, c)
                act.wait_ge(unit_done, u.done())
                act.wait_ge(ps_free[(u + 1).slot()], (u + 1).ps())
                fn(t_a[:, :], pp[u.slot()][:, :], ACT.Tanh, scale=0.5).then_inc(ps_free[u.slot()], 1)
                round_unit(u + 2)
                round_unit(u + 3)

            act.wait_ge(m_stored, 16 * KD)

            def decay_terms(g, o):
                scale, minus = sp2[:, ds(g * 3 + o, 1)], minus_sp4[:, ds(g * 3 + o, 1)]
                order.after(fn(lw[:, o, :], la[:, o, :], ACT.Exp, scale=minus, bias=minus))
                order.after(fn(la[:, o, :], la[:, o, :], ACT.Tanh, scale=scale, bias=scale))

            def root(o):
                fn(la[:, o, :], la[:, o, :], ACT.Sqrt).then_inc(lru_act, 1)

            def decay_of(g, u):
                round_unit(u + 1)
                decay_terms(g, 0)
                root(0)
                decay_terms(g, 1)
                decay_terms(g, 2)
                round_unit(u + 2)
                root(1)
                root(2)

            def gelu_gate(g, o):
                u = lru_unit(g, 3 + o)
                act.wait_ge(unit_done, u.done())
                fn(hl[:, ds(g * 3 + o, 1), :].rearrange("p a s -> p (a s)"),
                   pp[u.slot()][0:LT, :], ACT.Gelu_apprx_tanh).then_inc(ps_free[u.slot()], 1)

            def lru_group(g):
                for r in range(2, 7):
                    round_unit(lru_unit(g, r + 1))
                    if r >= 4:
                        gelu_gate(g, r - 4)
                for o in range(3):
                    u = lru_unit(g, 6)
                    if o == 2:
                        act.wait_ge(unit_done, u.done())
                        round_unit(lru_unit(g, 8))
                    else:
                        act.wait_ge(ra_ready, g * 2 + (o + 1))
                    fn(la[:, o, :], pp[2][0:LT, :], ACT.Tanh, scale=0.5,
                       bias=half_b[:, ds(g * 3 + o, 1)]).then_inc(ra_free, 1)
                    act.wait_ge(rx_ready, g * 3 + (o + 1))
                    fn(lc[:, o, :], pp[3][0:LT, :], ACT.Tanh, scale=0.5,
                       bias=half_b[:, ds(g * 3 + (o + LTILES), 1)]).then_inc(rx_free, 1)

            round_unit(lru_unit(0, 2))
            lru_group(0)
            with act.Fori(1, LGROUPS) as g:
                order.enter(g - 1, 3 * 2)
                decay_of(g - 1, lru_unit(g, 0))
                lru_group(g)
            order.leave(LGROUPS - 1)

            def merge_gate(u, c):
                act.wait_ge(unit_done, u.done())
                fn(t_b[:, ds(c, 1), :].rearrange("p a s -> p (a s)"), pp[u.slot()][:, :],
                   ACT.Tanh, scale=0.5).then_inc(ps_free[u.slot()], 1)

            decay_of(LGROUPS - 1, late_unit(U_GB))
            act.wait_ge(gated, LTILES)
            merge_gate(late_unit(U_GB), 0)
            merge_gate(late_unit(U_GB + 1), 1)
            act.wait_ge(lru_out, LTILES)
            with act.Fori(1, KD // 2) as c:
                for r in range(2):
                    u = late_unit(U_GB + r, 2, c)
                    round_unit(u + 1)
                    merge_gate(u, c * 2 + r)
            act.wait_ge(unit_done, U_YB)
            for k in range(LTILES):
                fn(hl_hi[:, k, :], hl[:, k, :], ACT.Copy).then_inc(hl_rounded, 1)
                if k == 3:
                    round_unit(late_unit(U_YB + 1))
            for r in range(1, 4):
                round_unit(late_unit(U_YB + r + 1))
            with act.Fori(1, KD // 2) as c:
                for r in range(4):
                    round_unit(late_unit(U_YB + r + 1, 4, c))

            def first_hi(raw, a_hi, u0, scale, ready):
                act.wait_ge(ready, 1)
                fn(a_hi[:, u0 % 2, :], raw[:, 0, 0:HALF], ACT.Copy, scale=scale).then_inc(a_rounded, 1)

            def contract(raw, a_hi, nk, u0, scale, ready, nth, last, square, seed_nth):
                for half in range(2):
                    def step(kk, r, more=True):
                        k = kk * 2 + r
                        u = late_unit(u0 + half * nk + r, 2, kk) if not isinstance(kk, int) else \
                            late_unit(u0 + half * nk + 2 * kk + r)
                        if half or r or not isinstance(kk, int):
                            if half == 0:
                                act.wait_ge(ready, k + 1)
                            act.wait_ge(unit_done, u.done(-1))
                            fn(a_hi[:, u.slot(), :], raw[:, ds(k, 1), half * HALF:(half + 1) * HALF].rearrange(
                                "p a s -> p (a s)"), ACT.Copy, scale=scale).then_inc(a_rounded, 1)
                        if more:
                            round_unit(u + 1)
                    if half:
                        for n in range(4):
                            step(n // 2, n % 2)
                            square(n)
                        rsqrt_seed(0, 4, seed_nth)
                    else:
                        step(0, 0)
                        step(0, 1)
                    end = nk // 2 - (1 if last and half else 0)
                    with act.Fori(1 + half, end) as kk:
                        step(kk, 0)
                        step(kk, 1)
                    if last and half:
                        step(end, 0)
                        step(end, 1, more=False)

            def square_stored(x_new, junk_, base):
                def square(i):
                    t = token_tile(i)
                    act.wait_ge(acc_stored, base - KD + i + 1)
                    act.wait_ge(squared, base + i)
                    fn(junk_[:, :], x_new[:, t, :], ACT.Square, accum_out=sumsq[:, t:t + 1]).then_inc(squared, 1)
                return square

            square2 = square_stored(x2, junk2, KD)
            first_hi(m, ao_hi, U_OUT, 0.5, m_ready)
            contract(m, ao_hi, KD, U_OUT, 0.5, m_ready, 0, False, square2, 3 + HEADS)
            norm_transposed(square2, x2, xn2, xr2, g_hi, KD, 2 + HEADS, 4 + HEADS, [ffn_unit(0) + 1])

            act.wait_ge(x2_saved, 16 * KD)

            def ffn_tile(j):
                u = ffn_unit(j)
                if not isinstance(j, int) or j:
                    round_unit(u + 1)
                act.wait_ge(unit_done, u.done())
                if not isinstance(j, int) or j:
                    act.wait_ge(hid_ready, j)
                fn(ug[:, :], pp[u.slot()][:, :], ACT.Identity, scale=vec_a[:, ds(j + A_W2, 1)],
                   bias=vec_a[:, ds(j + A_FB, 1)]).then_inc(u_first, 1)
                round_unit(u + 2)
                act.wait_ge(ps_free[u.slot()], u.ps(1))
                fn(ug[:, :], ug[:, :], ACT.Gelu_apprx_tanh).then_inc(u_gelu, 1)
                if isinstance(j, int) and j == FT - 1:
                    first_hi(hid, ad_hi, U_DN, 1.0, hid_ready)
                v = u + 1
                act.wait_ge(unit_done, v.done())
                fn(uv[:, :], pp[v.slot()][:, :], ACT.Identity, scale=vec_a[:, ds(j + (A_W2 + FT), 1)],
                   bias=vec_a[:, ds(j + (A_FB + FT), 1)]).then_inc(u_first, 1)

            ffn_tile(0)
            with act.Fori(1, FT - 1) as j:
                ffn_tile(j)
            ffn_tile(FT - 1)
            square3 = square_stored(y, junk, 2 * KD)
            contract(hid, ad_hi, FT, U_DN, 1.0, hid_ready, 2 * KD, True, square3, 5 + HEADS)

            for i in range(4, KD):
                square3(i)
            rsqrt_seed(4, 8, 6 + HEADS)

        @block.vector
        def _(dve):
            order = Order(dve, dve_order)
            after = order.after
            ts, tt, stt = nc.vector.tensor_scalar, nc.vector.tensor_tensor, nc.vector.scalar_tensor_tensor
            copy = nc.vector.tensor_copy

            def split_unit(u):
                dve.wait_ge(w_rounded, u.done())
                tt(w_lo[:, u.slot(), :], w_raw[:, u.slot(), :], f32(w_hi[:, u.slot(), :]),
                   ALU.subtract).then_inc(w_split, 1)

            def mean_square(n0, n1, width, sums):
                dve.wait_ge(*sums)
                ts(ms[:, n0:n1], sumsq[:, n0:n1], 1.0 / width, EPS, ALU.mult, ALU.add).then_inc(ms_ready, 1)

            def refine(n0, n1, nth):
                dve.wait_ge(ms_ready, nth)
                dve.wait_ge(rs0_ready, nth)
                after(tt(newton[:, n0:n1], rs[:, n0:n1], rs[:, n0:n1], ALU.mult))
                after(tt(newton[:, n0:n1], newton[:, n0:n1], ms[:, n0:n1], ALU.mult))
                after(ts(newton[:, n0:n1], newton[:, n0:n1], -0.5, 1.5, ALU.mult, ALU.add))
                tt(rs[:, n0:n1], rs[:, n0:n1], newton[:, n0:n1], ALU.mult).then_inc(rs_ready, 1)
                dve.wait_ge(rs_ready, nth)

            def rsqrt(n0, n1, width, sums, nth):
                mean_square(n0, n1, width, sums)
                refine(n0, n1, nth)

            def norm_transposed(xr, gain0, dst_hi, dst_lo, base, nth, units):
                gain = vec_a[:, gain0:gain0 + KD].unsqueeze(2).broadcast_to([P, KD, P])
                for t in range(KD):
                    if t == 2:
                        mean_square(4, 8, D, (squared, base + KD))
                    dve.wait_ge(xT_ready, base + t + 1)
                    tt(xr[:, t % 2, :].rearrange("p (k c) -> p k c", c=P),
                       pp[2 + t % 2][:, :].rearrange("p (k c) -> p k c", c=P), gain, ALU.mult).then_inc(xr_ready, 1)
                    if t == 2:
                        refine(4, 8, nth)
                    dve.wait_ge(xr_ready, base + t + 1)
                    dve.wait_ge(xr_rounded, base + t + 1)
                    tt(dst_lo[:, :, t * P:(t + 1) * P], xr[:, t % 2, :].rearrange("p (k c) -> p k c", c=P),
                       f32(dst_hi[:, :, t * P:(t + 1) * P]), ALU.subtract).then_inc(xT_split, 1)
                    if t in (2, 3) and t - 2 >= 2 - len(units):
                        split_unit(units[t - 4])
                dve.wait_ge(xT_split, base + KD)

            rsqrt(0, 4, D, (squared, 4), 1)
            dve.wait_ge(vecs_T, 3)
            copy(vec_a[:, :], pp[0][:, 0:N_A]).then_inc(vecs, 1)
            copy(vec_b[:, :], pp[1][:, 0:N_B]).then_inc(vecs, 1)
            copy(vec_l[:, :], pp[2][0:LT, 0:N_L]).then_inc(vecs, 1)
            dve.wait_ge(vecs, 3)
            ts(onorm_half[:, :], vec_a[:, A_ONORM:A_FNORM], 0.5, None, ALU.mult)
            ts(half_b[:, :], vec_l[:, L_BA:L_AP], 0.5, None, ALU.mult)
            norm_transposed(xr1, A_NORM, h_hi, h_lo, 0, 2, [Unit(U_F), Unit(U_QKV0)])

            e, s, z, poly = (soft[:, n, :] for n in range(4))
            dve.wait_ge(soft_e, 1)
            after(ts(s, e, 2.0, None, ALU.add))
            after(nc.vector.reciprocal(s, s))
            after(tt(s, s, e, ALU.mult))
            after(tt(z, s, s, ALU.mult))
            after(ts(poly, z, 1.0 / 17, 1.0 / 15, ALU.mult, ALU.add))
            for n in (13, 11, 9, 7, 5, 3, 1):
                after(tt(poly, poly, z, ALU.mult))
                after(ts(poly, poly, 1.0 / n, None, ALU.add))
            after(tt(poly, poly, s, ALU.mult))
            after(ts(z, vec_l[:, L_AP:N_L], 0.0, 2.0, ALU.max, ALU.mult))
            after(stt(sp2[:, :], poly, 4.0, z, ALU.mult, ALU.add))
            ts(minus_sp4[:, :], sp2[:, :], -2.0, None, ALU.mult)

            dve.wait_ge(setup, 12)

            dve.wait_ge(rows_loaded, 16 * 13)
            dve.wait_ge(unit_done, 1)
            after(copy(f_hi[:, :], pp[0][0:RANK, :]))
            tt(f_lo[:, :], pp[0][0:RANK, :], f32(f_hi[:, :]), ALU.subtract).then_inc(ps_free[0], 1)

            def forget_weights(h):
                part = wf_raw[:, ds(h * DK, DK)]
                after(copy(wf_hi[:, :], part))
                tt(wf_lo[:, :], part, f32(wf_hi[:, :]), ALU.subtract).then_inc(wf_ready, 1)

            def gla_qkv(u, h, final):
                bias = vec_a[:, ds(h + A_BF2, 1)]
                split_unit(u + 1)
                dve.wait_ge(z_abs, h + 1)
                ts(cum[:, :], pp[2][:, :], bias, 0.0, ALU.add, ALU.min).then_inc(z_free, 1)
                dve.wait_ge(z_free, h + 1)
                dve.wait_ge(sp_ready, h + 1)
                after(tt(cum[:, :], cum[:, :], g1[:, :], ALU.subtract))
                for n in range(S // CHUNK):
                    part = cum[:, n * CHUNK:(n + 1) * CHUNK]
                    scan = nc.vector.tensor_tensor_scan(part, ones[:, :], part, 0.0, ALU.mult, ALU.add)
                scan.then_inc(cum_ready, 1)
                dve.wait_ge(cum_ready, h + 1)
                by_chunk = cum[:, :].rearrange("p (n c) -> p n c", c=CHUNK)
                tt(ks[:, :].rearrange("p (n c) -> p n c", c=CHUNK),
                   by_chunk[:, :, CHUNK - 1:CHUNK].broadcast_to([P, S // CHUNK, CHUNK]), by_chunk,
                   ALU.subtract).then_inc(bdiff_ready, 1)
                if final:
                    rsqrt(0, PAIRS, DV, (o_stored, h * PAIRS), h + 2)
                    tt(vo[:, :, :], vo[:, :, :], rs[:, :].unsqueeze(2).broadcast_to([P, PAIRS, DV]),
                       ALU.mult).then_inc(on_ready, 1)
                dve.wait_ge(gates_ready, h * 3 + 1)
                dve.wait_ge(unit_done, u.done())
                stt(g1[:, :], pp[u.slot()][:, :], DK ** -0.5, g1[:, :], ALU.mult, ALU.mult).then_inc(ps_free[u.slot()], 1)
                dve.wait_ge(qk_rounded, h * 2 + 1)
                for c in range(2):
                    tt(q_chunks(q_lo, c), chunks(g1, c), f32(q_chunks(q_hi, c)), ALU.subtract)
                split_unit(u + 2)
                k = u + 1
                dve.wait_ge(gates_ready, h * 3 + 3)
                dve.wait_ge(unit_done, k.done())
                tt(g2[:, :], pp[k.slot()][:, :], g2[:, :], ALU.mult)
                tt(ks[:, :], pp[k.slot()][:, :], ks[:, :], ALU.mult).then_inc(ps_free[k.slot()], 1)
                dve.wait_ge(qk_rounded, h * 2 + 2)
                tt(k_lo[:, :], g2[:, :], f32(k_hi[:, :]), ALU.subtract).then_inc(qk_split, 1)
                split_unit(u + 3)
                if final:
                    gla_final(h - 1)
                split_unit(u + 4)

            def gla_final(h):
                for d, ps in ((0, pp[3]), (1, pp[2])):
                    dve.wait_ge(oT_ready, h * 2 + (d + 1))
                    stt(og_raw[:, ds(h * 2 + d, 1), :].rearrange("p a s -> p (a s)"), ps[:, :],
                        onorm_half[:, d:d + 1], sg[:, d, :], ALU.mult, ALU.mult).then_inc(og_ready, 1)

            def gla_gate(u, h, d):
                dve.wait_ge(g_tanh, h * 2 + (d + 1))
                stt(sg[:, d, :], sg[:, d, :], 1.0, pp[(u + d).slot()][:, :], ALU.add,
                    ALU.mult).then_inc(ps_free[(u + d).slot()], 1)

            def gla_steps(u, h, more=True):
                nc.vector.memset(s_raw[:, :], 0.0)
                nc.vector.memset(f32(s_hi[:, 0, :]), 0.0)
                nc.vector.memset(f32(s_lo[:, 0, :]), 0.0).then_inc(s_cleared, 1)
                dve.wait_ge(s_cleared, h + 1)

                def split_kv(p):
                    dve.wait_ge(kv_rounded, h * PAIRS + (p + 1))
                    for c in range(2):
                        rows = slice(c * CHUNK, (c + 1) * CHUNK)
                        tt(kt_lo[rows, c, :], tr_ps[rows, 0:P], f32(kt_hi[rows, c, :]), ALU.subtract)
                    if p == 0:
                        dve.wait_ge(at_ready, h * PAIRS + 1)
                    tt(v_lo[:, p % 2, :], tr_ps[:, P:], f32(v_hi[:, p % 2, :]), ALU.subtract).then_inc(kv_split, 1)

                split_kv(0)
                for p in range(PAIRS):
                    n = h * PAIRS + p
                    nc.vector.copy_predicated(at_raw[:, :], causal[:, :].bitcast(mybir.dt.uint32),
                                              at_ps).then_inc(at_masked, 1)
                    dve.wait_ge(at_rounded, n + 1)
                    tt(at_lo[:, :], at_raw[:, :], f32(at_hi[:, :]), ALU.subtract).then_inc(at_split, 1)
                    dve.wait_ge(ds_ready, n + 1)
                    for c in range(2):
                        slot = 1 - c
                        stt(s_raw[:, :], s_raw[:, :], decay[:, 2 * p + c:2 * p + c + 1],
                            ds_ps[:, c * DV:(c + 1) * DV], ALU.mult, ALU.add).then_inc(s_updated, 1)
                        if c:
                            if p + 1 < PAIRS:
                                split_kv(p + 1)
                            if p % 4 == 0:
                                split_unit(u + (1 + p // 4))
                            if p == 5:
                                gla_gate(u, h, 0)
                            if p == 6 and more:
                                forget_weights(h + 1)
                            if p + 1 < PAIRS:
                                dve.wait_ge(at_ready, n + 2)
                        dve.wait_ge(s_updated, n * 2 + (c + 1))
                        dve.wait_ge(s_rounded, n * 2 + (c + 1))
                        tt(s_lo[:, slot, :], s_raw[:, :], f32(s_hi[:, slot, :]), ALU.subtract).then_inc(s_split, 1)
                gla_gate(u, h, 1)

            forget_weights(0)
            gla_qkv(Unit(U_QKV0), 0, False)
            with dve.Fori(0, HEADS - 1) as h:
                order.enter(h, 1 + 1 + 3)
                gla_steps(Unit(U_HEAD, 6, h), h)
                gla_qkv(Unit(U_HEAD + 2, 6, h), h + 1, True)
            order.leave(HEADS - 1)
            gla_steps(Unit(U_G3), HEADS - 1, more=False)
            rsqrt(0, PAIRS, DV, (o_stored, HEADS * PAIRS), 2 + HEADS)
            tt(vo[:, :, :], vo[:, :, :], rs[:, :].unsqueeze(2).broadcast_to([P, PAIRS, DV]),
               ALU.mult).then_inc(on_ready, 1)

            split_unit(Unit(U_YA + 1))
            for k in range(2 * HEADS):
                if k == 2 * (HEADS - 1):
                    gla_final(HEADS - 1)
                    dve.wait_ge(og_ready, 2 * HEADS)
                dve.wait_ge(og_rounded, k + 1)
                tt(og_lo[:, k, :], og_raw[:, k, :], f32(og_hi[:, k, :]), ALU.subtract).then_inc(og_split, 1)
            with dve.Fori(0, KD) as c:
                u = Unit(U_YA, 2, c)
                wo = u + 1
                split_unit(u + 2)
                split_unit(u + 3)
                dve.wait_ge(ps_free[u.slot()], u.ps(1))
                dve.wait_ge(unit_done, wo.done())
                stt(m_a[:, ds(c, 1), :].rearrange("p a s -> p (a s)"), t_a[:, :], 1.0,
                    pp[wo.slot()][:, :], ALU.add, ALU.mult).then_inc(ps_free[wo.slot()], 1)

            dve.wait_ge(m_stored, 16 * KD)

            def convolve(g, r):
                u = lru_unit(g, r)
                ps = pp[u.slot()]

                def col(at):
                    return vec_l[:, ds(g * 3 + (at + r), 1)]

                dve.wait_ge(unit_done, u.done())
                if r:
                    dve.wait_ge(xc_split, g * 3 + r)
                after(ts(conv[:, :], ps[0:LT, :], col(L_W + 3 * LTILES), col(L_B), ALU.mult, ALU.add))
                after(stt(conv[:, 1:], ps[0:LT, :S - 1], col(L_W + 2 * LTILES), conv[:, 1:], ALU.mult, ALU.add))
                after(stt(conv[:, 2:], ps[0:LT, :S - 2], col(L_W + LTILES), conv[:, 2:], ALU.mult, ALU.add))
                stt(conv[:, 3:], ps[0:LT, :S - 3], col(L_W), conv[:, 3:], ALU.mult,
                    ALU.add).then_inc(ps_free[u.slot()], 1)
                dve.wait_ge(ps_free[u.slot()], u.ps(1))
                after(copy(xc_hi[:, r, :], conv[:, :]))
                tt(xc_lo[:, r, :], conv[:, :], f32(xc_hi[:, r, :]), ALU.subtract).then_inc(xc_split, 1)

            def gated_input(g, o):
                C = lc[:, o, :]
                dve.wait_ge(rx_free, g * 3 + (o + 1))
                after(tt(conv[:, :], f32(xc_hi[:, o, :]), f32(xc_lo[:, o, :]), ALU.add))
                stt(C, C, 1.0, conv[:, :], ALU.add, ALU.mult).then_inc(gated, 1)
                dve.wait_ge(gated, g * 3 + (o + 1))

            def recur(g, o):
                A, B, C = lw[:, o, :], la[:, o, :], lc[:, o, :]
                gate = lru_unit(g, 3 + o)
                dve.wait_ge(lru_act, g * 3 + (o + 1))
                after(stt(B, A, 1.0, B, ALU.add, ALU.mult))
                after(stt(B, B, 0.5, C, ALU.mult, ALU.mult))
                after(nc.vector.tensor_tensor_scan(C, A, B, 0.0, ALU.mult, ALU.add))
                dve.wait_ge(ps_free[gate.slot()], gate.ps(1))
                out_tile = hl[:, ds(g * 3 + o, 1), :].rearrange("p a s -> p (a s)")
                tt(out_tile, out_tile, C, ALU.mult).then_inc(lru_out, 1)

            def lru_group(g, before):
                before(0)
                for r in range(3):
                    split_unit(lru_unit(g, r + 2))
                    convolve(g, r)
                for r in (5, 6):
                    split_unit(lru_unit(g, r))
                    before(r - 4)
                split_unit(lru_unit(g, 7))
                gated_input(g, 0)
                gated_input(g, 1)
                split_unit(lru_unit(g, 8))
                gated_input(g, 2)

            lru_group(0, lambda o: None)
            with dve.Fori(1, LGROUPS) as g:
                order.enter(g - 1, 3 * 4 + 3 + 3 * 3)
                split_unit(lru_unit(g, 1))
                lru_group(g, lambda o: recur(g - 1, o))
            order.leave(LGROUPS - 1)
            for o in range(3):
                if o < 2:
                    split_unit(late_unit(U_GB + o + 1))
                recur(LGROUPS - 1, o)

            for n in range(2, KD):
                split_unit(late_unit(U_GB + n + 1))
            for k in range(LTILES):
                dve.wait_ge(hl_rounded, k + 1)
                tt(hl_lo[:, k, :], hl[:, k, :], f32(hl_hi[:, k, :]), ALU.subtract).then_inc(hl_split, 1)
                if k == 3:
                    split_unit(late_unit(U_YB + 1))

            def branch_b(i, n, u):
                c = i * 2 + n
                dve.wait_ge(unit_done, u.done())
                stt(yb[:, :], t_b[:, ds(c, 1), :].rearrange("p a s -> p (a s)"), 1.0, pp[2 + n][:, :],
                    ALU.add, ALU.mult).then_inc(yb_free[n], 1)
                dve.wait_ge(yb_free[n], i + 1)
                merged = m[:, ds(c, 1), :].rearrange("p a s -> p (a s)")
                tt(merged, merged, yb[:, :], ALU.add).then_inc(m_ready, 1)
                dve.wait_ge(m_ready, c + 1)

            dve.wait_ge(m_loaded, 16)
            for r in range(1, 4):
                split_unit(late_unit(U_YB + r + 1))
                if r == 1:
                    branch_b(0, 0, late_unit(U_YB + 1))
            branch_b(0, 1, late_unit(U_YB + 3))
            with dve.Fori(1, KD // 2 - 1) as c:
                u = late_unit(U_YB, 4, c)
                for n in range(2):
                    split_unit(u + (2 * n + 1))
                    split_unit(u + (2 * n + 2))
                    branch_b(c, n, u + (2 * n + 1))

            def first_lo(raw, a_hi, a_lo, u0, scale, nth):
                slot = u0 % 2
                dve.wait_ge(a_rounded, nth + 1)
                stt(a_lo[:, slot, :], raw[:, 0, 0:HALF], scale, f32(a_hi[:, slot, :]), ALU.mult,
                    ALU.subtract).then_inc(a_split, 1)

            u = late_unit(U_OUT - 4)
            for n in range(2):
                split_unit(u + (2 * n + 1))
                split_unit(u + (2 * n + 2))
                if n:
                    first_lo(m, ao_hi, ao_lo, U_OUT, 0.5, 0)
                branch_b(KD // 2 - 1, n, u + (2 * n + 1))

            def contract(raw, a_hi, a_lo, nk, u0, scale, nth, last, residual, loaded, peel, beside):
                for half in range(2):
                    def split_act(kk, r):
                        k = kk * 2 + r
                        slot = (u0 + r) % 2
                        dve.wait_ge(a_rounded, k + (nth + half * nk + 1))
                        stt(a_lo[:, slot, :], raw[:, ds(k, 1), half * HALF:(half + 1) * HALF].rearrange(
                            "p a s -> p (a s)"), scale, f32(a_hi[:, slot, :]), ALU.mult,
                            ALU.subtract).then_inc(a_split, 1)

                    def unit(kk, r):
                        return late_unit(u0 + half * nk + 2 * kk + r) if isinstance(kk, int) else \
                            late_unit(u0 + half * nk + r, 2, kk)

                    def store(half):
                        for i in range(4):
                            if i < 3:
                                dve.wait_ge(tile_done, 3 * (nth // KD + half) + i + 1)
                            else:
                                dve.wait_ge(unit_done, u0 + (half + 1) * nk)
                            t = token_tile(4 * half + i)
                            tt(residual[:, t, :], pp[t % 4][:, :], residual[:, t, :],
                               ALU.add).then_inc(acc_stored, 1)

                    if half:
                        split_act(0, 0)
                        store(0)
                    split_unit(unit(0, 1))
                    split_act(0, 1)
                    split_unit(unit(0, 2))
                    end = nk // 2 - (1 if last and half else 0)
                    for n in range(2, 2 * peel if half else 2):
                        split_act(n // 2, n % 2)
                        split_unit(unit(n // 2, n % 2 + 1))
                        beside(n)
                    with dve.Fori(peel if half else 1, end) as kk:
                        for r in range(2):
                            split_act(kk, r)
                            split_unit(unit(kk, r + 1))
                    if last and half:
                        split_act(end, 0)
                        split_unit(unit(end, 1))
                        split_act(end, 1)
                    dve.wait_ge(loaded[half][0], 16 * loaded[half][1])
                store(1)
                dve.wait_ge(acc_stored, nth // (2 * KD) * KD + KD)

            def beside_out(n):
                if n == 3:
                    mean_square(0, 4, D, (squared, KD + 4))
                if n == 4:
                    refine(0, 4, 3 + HEADS)

            contract(m, ao_hi, ao_lo, KD, U_OUT, 0.5, 0, False, x2,
                     [(xres_loaded[0], 4), (xres_loaded[1], 4)], 3, beside_out)
            norm_transposed(xr2, A_FNORM, g_hi, g_lo, KD, 4 + HEADS, [ffn_unit(0) + 1])

            dve.wait_ge(x2_saved, 16 * KD)

            def ffn_tile(j):
                u = ffn_unit(j)
                for n, acc in ((0, ug), (1, uv)):
                    if n or not isinstance(j, int) or j:
                        split_unit(u + (n + 1))
                    if n and isinstance(j, int) and j:
                        first_lo(hid, ad_hi, ad_lo, U_DN, 1.0, 2 * KD)
                    ps = pp[(u + n).slot()]
                    dve.wait_ge(u_first, j * 2 + (n + 1))
                    after(stt(acc[:, 1:], ps[:, :S - 1], vec_b[:, ds(j + (2 + n) * FT, 1)], acc[:, 1:],
                              ALU.mult, ALU.add))
                    stt(acc[:, 2:], ps[:, :S - 2], vec_b[:, ds(j + n * FT, 1)], acc[:, 2:],
                        ALU.mult, ALU.add).then_inc(ps_free[(u + n).slot()], 1)
                dve.wait_ge(ps_free[(u + 1).slot()], (u + 1).ps(1))
                dve.wait_ge(u_gelu, j + 1)
                tt(hid[:, ds(j, 1), :].rearrange("p a s -> p (a s)"), ug[:, :], uv[:, :],
                   ALU.mult).then_inc(hid_ready, 1)

            ffn_tile(0)
            with dve.Fori(1, FT - 1) as j:
                order.enter(j - 1, 2)
                ffn_tile(j)
            order.leave(FT - 2)
            ffn_tile(FT - 1)

            def beside_down(n):
                if n == 3:
                    mean_square(0, 4, D, (squared, 2 * KD + 4))
                if n == 4:
                    refine(0, 4, 5 + HEADS)
                if 5 <= n < 9:
                    t = token_tile(n - 5)
                    stt(y[:, t, :], y[:, t, :], rs[:, t:t + 1], final_gain[:, :], ALU.mult,
                        ALU.mult).then_inc(y_ready, 1)

            contract(hid, ad_hi, ad_lo, FT, U_DN, 1.0, 2 * KD, True, y,
                     [(x2_loaded[0], 5), (x2_loaded[1], 4)], 5, beside_down)
            for i in range(4, KD):
                t = token_tile(i)
                dve.wait_ge(squared, 2 * KD + i + 1)
                after(tt(y[:, t, :], y[:, t, :], final_gain[:, :], ALU.mult))
            rsqrt(4, 8, D, (squared, 3 * KD), 6 + HEADS)
            for i in range(4, KD):
                t = token_tile(i)
                ts(y[:, t, :], y[:, t, :], rs[:, t:t + 1], None, ALU.mult).then_inc(y_ready, 1)

        @block.tensor
        def _(pe):
            mm = nc.tensor.matmul

            def split_product(dst, s_hi_, s_lo_, m_hi_, m_lo_, start, stop):
                mm(dst, s_hi_, m_hi_, start=start, stop=False)
                mm(dst, s_hi_, m_lo_, start=False, stop=False)
                return mm(dst, s_lo_, m_hi_, start=False, stop=stop)

            def weights(u, k, n=P, rows=P):
                return (w_hi[0:rows, u.slot(), k * n:(k + 1) * n], w_lo[0:rows, u.slot(), k * n:(k + 1) * n])

            def begin(u):
                pe.wait_ge(w_split, u.done())
                if not (u.i is None and u.ps() == 0):
                    pe.wait_ge(ps_free[u.slot()], u.ps())

            def project(u, a_hi, a_lo, n=P, parts=range(8), wait_k=None):
                if 0 in parts:
                    begin(u)
                for part in parts:
                    half, k0 = part // 4, 2 * (part % 4)
                    for k in (k0, k0 + 1):
                        if wait_k and half == 0:
                            pe.wait_ge(wait_k, k + 1)
                        tok = slice(half * HALF, (half + 1) * HALF)
                        last = split_product(pp[u.slot()][0:n, tok], *weights(u, k, n), a_hi[:, k, tok],
                                             a_lo[:, k, tok], k == 0, k == KD - 1)
                if 7 in parts:
                    last.then_inc(unit_done, 1)

            def norm_transposed(xn, base, free, first, second, a_hi, a_lo):
                for t in range(KD):
                    pe.wait_ge(xn_ready, base + t + 1)
                    if t >= 2:
                        pe.wait_ge(xr_ready, base + t - 1)
                    elif free:
                        pe.wait_ge(free[0], free[1] + t)
                    for k in range(KD):
                        last = nc.tensor.transpose(pp[2 + t % 2][:, k * P:(k + 1) * P],
                                                   xn[:, t % 2, k * P:(k + 1) * P], ident[:, :])
                    last.then_inc(xT_ready, 1)
                    if t >= 4:
                        pe.wait_ge(xT_split, base + 4)
                        project(first[0], a_hi, a_lo, n=first[1], parts=[t - 4])
                project(second[0], a_hi, a_lo, n=second[1], parts=range(4))
                pe.wait_ge(xT_split, base + KD)
                project(first[0], a_hi, a_lo, n=first[1], parts=range(4, 8))

            pe.wait_ge(setup, 7)
            pe.wait_ge(rows_loaded, 16 * 13)
            nc.tensor.transpose(pp[0][:, 0:N_A], rows_a[:, :], ident[0:N_A, 0:N_A]).then_inc(vecs_T, 1)
            nc.tensor.transpose(pp[1][:, 0:N_B], rows_b[:, :], ident[0:N_B, 0:N_B]).then_inc(vecs_T, 1)
            nc.tensor.transpose(pp[2][0:LT, 0:N_L], rows_l[:, :], ident[0:N_L, 0:N_L]).then_inc(vecs_T, 1)
            pe.wait_ge(vecs, 3)
            norm_transposed(xn1, 0, None, (Unit(U_F), RANK), (Unit(U_QKV0), P), h_hi, h_lo)

            def gla_qkv(u, h, final):
                before = range(2) if final else range(4, 6)
                project(u, h_hi, h_lo, parts=before)
                pe.wait_ge(wf_ready, h + 1)
                if final:
                    pe.wait_ge(o_stored, h * PAIRS)
                else:
                    pe.wait_ge(ps_free[0], 1)
                for half in range(2):
                    tok = slice(half * HALF, (half + 1) * HALF)
                    last = split_product(pp[2][:, tok], wf_hi[:, :], wf_lo[:, :], f_hi[:, tok], f_lo[:, tok],
                                         True, True)
                last.then_inc(z_ready, 1)
                project(u, h_hi, h_lo, parts=range(before.stop, 8))
                project(u + 1, h_hi, h_lo)
                if final:
                    gla_final(h - 1)
                project(u + 2, h_hi, h_lo)
                project(u + 3, h_hi, h_lo)

            def gla_final(h):
                pe.wait_ge(on_ready, h + 1)
                pe.wait_ge(s_updated, (h + 1) * (2 * PAIRS))
                for d, ps in ((0, pp[3]), (1, pp[2])):
                    for p in range(PAIRS):
                        last = nc.tensor.transpose(ps[:, p * P:(p + 1) * P], vo[:, p, d * P:(d + 1) * P], ident[:, :])
                    last.then_inc(oT_ready, 1)

            def gla_steps(u, h):
                def gate_part(i):
                    project(u + i // 8, h_hi, h_lo, parts=[i % 8])

                def transpose_kv(p):
                    tok = slice(p * P, (p + 1) * P)
                    nc.tensor.transpose(tr_ps[:, 0:P], ks[:, tok], ident[:, :])
                    nc.tensor.transpose(tr_ps[:, P:2 * P], vo[:, p, 0:P], ident[:, :])
                    nc.tensor.transpose(tr_ps[:, 2 * P:], vo[:, p, P:], ident[:, :]).then_inc(tr_ready, 1)

                gate_part(0)
                pe.wait_ge(qk_split, h + 1)
                for v in (0, 1):
                    w = u + (v - 2)
                    pe.wait_ge(ps_free[w.slot()], w.ps(1))
                pe.wait_ge(z_free, h + 1)
                transpose_kv(0)
                for p in range(PAIRS):
                    n = h * PAIRS + p
                    tok = slice(p * P, (p + 1) * P)
                    if p:
                        pe.wait_ge(at_masked, n)
                    split_product(at_ps, k_hi[:, tok], k_lo[:, tok], gla_q_tokens(q_hi, p), gla_q_tokens(q_lo, p),
                                  True, True).then_inc(at_ready, 1)
                    if p + 1 < PAIRS:
                        gate_part(2 * p + 1)
                    pe.wait_ge(kv_split, n + 1)
                    if p:
                        pe.wait_ge(s_updated, n * 2)
                    for c in range(2):
                        last = split_product(ds_ps[:, c * DV:(c + 1) * DV], kt_hi[:, c, :], kt_lo[:, c, :],
                                             v_hi[:, p % 2, :], v_lo[:, p % 2, :], True, True)
                    last.then_inc(ds_ready, 1)
                    if p + 1 < PAIRS:
                        transpose_kv(p + 1)
                    gate_part(min(2 * p + 2, 2 * PAIRS - 1))
                    if p:
                        pe.wait_ge(o_stored, n)
                    pe.wait_ge(at_split, n + 1)
                    split_product(o_ps, at_hi[:, :], at_lo[:, :], v_hi[:, p % 2, :], v_lo[:, p % 2, :], True, False)
                    if p:
                        pe.wait_ge(s_split, n * 2)
                    else:
                        pe.wait_ge(s_cleared, h + 1)
                    split_product(o_ps, gla_q(q_hi, p, 0), gla_q(q_lo, p, 0), s_hi[:, 0, :], s_lo[:, 0, :], False, False)
                    pe.wait_ge(s_split, n * 2 + 1)
                    split_product(o_ps, gla_q(q_hi, p, 1), gla_q(q_lo, p, 1), s_hi[:, 1, :], s_lo[:, 1, :],
                                  False, True).then_inc(o_ready, 1)

            gla_qkv(Unit(U_QKV0), 0, False)
            with pe.Fori(0, HEADS - 1) as h:
                gla_steps(Unit(U_HEAD, 6, h), h)
                gla_qkv(Unit(U_HEAD + 2, 6, h), h + 1, True)
            gla_steps(Unit(U_G3), HEADS - 1)

            project(Unit(U_YA), h_hi, h_lo)
            gla_final(HEADS - 1)
            project(Unit(U_YA + 1), og_hi, og_lo, wait_k=og_split)
            with pe.Fori(1, KD) as c:
                u = Unit(U_YA, 2, c)
                project(u, h_hi, h_lo)
                project(u + 1, og_hi, og_lo)

            with pe.Fori(0, LGROUPS) as g:
                for r in range(6):
                    project(lru_unit(g, r), h_hi, h_lo, n=LT)
                wa, wx = lru_unit(g, 6), lru_unit(g, 7)
                pe.wait_ge(xc_split, g * 3 + 3)
                for o in range(3):
                    tiles = range(max(0, o - 1), min(2, o + 1) + 1)
                    for u, ps, ready, free in ((wa, pp[2], ra_ready, ra_free), (wx, pp[3], rx_ready, rx_free)):
                        if o:
                            pe.wait_ge(free, g * 3 + o)
                        else:
                            pe.wait_ge(w_split, u.done())
                        for half in range(2):
                            tok = slice(half * HALF, (half + 1) * HALF)
                            for k in tiles:
                                c0 = k * 3 * LT + o * LT
                                last = split_product(
                                    ps[0:LT, tok], w_hi[0:LT, u.slot(), c0:c0 + LT], w_lo[0:LT, u.slot(), c0:c0 + LT],
                                    xc_hi[:, k, tok], xc_lo[:, k, tok], k == tiles[0], k == tiles[-1])
                        if u is wa and o == 2:
                            last.then_inc(unit_done, 1)
                        else:
                            last.then_inc(ready, 1)
                pe.wait_ge(rx_ready, g * 3 + 3)
                pe.sem_inc(unit_done, 1)

            with pe.Fori(0, KD // 2) as c:
                for r in range(2):
                    project(late_unit(U_GB + r, 2, c), h_hi, h_lo)
            pe.wait_ge(rx_free, LTILES)
            with pe.Fori(0, KD // 2) as c:
                for n in range(2):
                    for r in range(2):
                        u = late_unit(U_YB + 2 * n + r, 4, c)
                        pe.wait_ge(w_split, u.done())
                        for k in range(6):
                            pe.wait_ge(hl_split, 6 * r + k + 1)
                            for half in range(2):
                                tok = slice(half * HALF, (half + 1) * HALF)
                                last = split_product(pp[2 + n][:, tok], *weights(u, k, P, LT), hl_hi[:, 6 * r + k, tok],
                                                     hl_lo[:, 6 * r + k, tok], r + k == 0, r == 1 and k == 5)
                        last.then_inc(unit_done, 1)

            def contract(a_hi, a_lo, nk, u0, nth, free):
                for half in range(2):
                    def step(kk, r, first=False, final=False):
                        u = late_unit(u0 + half * nk + 2 * kk + r) if isinstance(kk, int) else \
                            late_unit(u0 + half * nk + r, 2, kk)
                        pe.wait_ge(w_split, u.done())
                        pe.wait_ge(a_split, kk * 2 + (nth + half * nk + r + 1))
                        for i in range(4):
                            t = token_tile(i)
                            if first and half:
                                pe.wait_ge(acc_stored, nth // (2 * KD) * KD + i + 1)
                            elif first:
                                for wait in free[t]:
                                    pe.wait_ge(*wait)
                            tok = slice(t * P, (t + 1) * P)
                            for c in range(2):
                                col = slice(c * HALF, (c + 1) * HALF)
                                last = split_product(
                                    pp[t][:, col], a_hi[:, u.slot(), tok], a_lo[:, u.slot(), tok],
                                    w_hi[:, u.slot(), col], w_lo[:, u.slot(), col], first, final)
                            if i == 3:
                                last.then_inc(unit_done, 1)
                            elif final:
                                last.then_inc(tile_done, 1)
                    step(0, 0, first=True)
                    step(0, 1)
                    with pe.Fori(1, nk // 2 - 1) as kk:
                        step(kk, 0)
                        step(kk, 1)
                    step(nk // 2 - 1, 0)
                    step(nk // 2 - 1, 1, final=True)

            contract(ao_hi, ao_lo, KD, U_OUT, 0,
                     [[(ps_free[0], gb_uses(0))], [(ps_free[1], gb_uses(1))], [(yb_free[0], 4)], [(yb_free[1], 4)]])
            norm_transposed(xn2, KD, (acc_stored, 5), (ffn_unit(0), P), (ffn_unit(0) + 1, P), g_hi, g_lo)
            project(ffn_unit(0) + 1, g_hi, g_lo, parts=range(4, 8))

            with pe.Fori(1, FT) as j:
                for n in range(2):
                    project(late_unit(U_UP + n, 2, j, apart=LGROUPS + 2 * KD), g_hi, g_lo)
            up_uses = [gb_uses(n) + FT for n in range(2)]
            contract(ad_hi, ad_lo, FT, U_DN, 2 * KD,
                     [[(ps_free[0], up_uses[0])], [(ps_free[1], up_uses[1])], [], []])


_INS = ["x", "attn_norm", "w_in", "gla_wf2", "gla_bf2", "gla_onorm", "gla_wo", "lru_conv_w", "lru_conv_b",
        "lru_wa", "lru_ba", "lru_wx", "lru_bx", "lru_a_param", "lru_wo", "w_out", "ffn_norm", "ffn_wup",
        "ffn_conv_w", "ffn_conv_b", "ffn_wdown", "final_norm"]


def kernel(**inputs):
    import numpy as _np
    import concourse.bacc as _bacc
    from concourse import mybir as _mybir
    from concourse.bass_utils import run_bass_kernel_spmd as _run

    nc = _bacc.Bacc("TRN2", target_bir_lowering=False, num_devices=1)
    arrays, args = {}, []
    for name in _INS:
        a = _np.ascontiguousarray(inputs[name])
        arrays[f"in_{name}_dram"] = a
        args.append(nc.dram_tensor(f"in_{name}_dram", a.shape, _mybir.dt.from_np(a.dtype), kind="ExternalInput").ap())
    out = nc.dram_tensor("out_dram", (1, S, D), _mybir.dt.float32, kind="ExternalOutput").ap()
    build(nc, *args, out)
    r = _run(nc, [arrays], core_ids=[0])
    return r.results[0]["out_dram"]
```
